# Optimizing a Trainium2 kernel written in Bass

```python
import jax, jax.numpy as jnp
from jax import lax
import numpy as np
import math

D_MODEL = 1024
BATCH = 1
SEQ = 512
DEPTH = 1

HEAD_DIM = 64
FOX_HEADS = 8
SWA_HEADS = 8
SWA_KV_HEADS = 2
SWA_GROUP = SWA_HEADS // SWA_KV_HEADS
WINDOW = 128
Q_BLOCK = 128
ROPE_THETA = 10000.0
N_GROUPS = 8
EXPERTS_PER_GROUP = 8
N_EXPERTS = N_GROUPS * EXPERTS_PER_GROUP
TOP_K = 2
D_EXPERT = D_MODEL // 2
MOE_BLOCK = 128
EPS = 1e-6

FOX_W = FOX_HEADS * HEAD_DIM
SWA_W = SWA_HEADS * HEAD_DIM
SWA_KV_W = SWA_KV_HEADS * HEAD_DIM
IN_SPLITS = (FOX_W, FOX_W, FOX_W, FOX_HEADS, SWA_W, SWA_KV_W, SWA_KV_W, D_MODEL, D_MODEL)
N_IN = sum(IN_SPLITS)
SPLIT_POINTS = tuple(int(v) for v in np.cumsum(IN_SPLITS)[:-1])


def rms_norm(x, g):
    xf = x.astype(jnp.float32)
    y = xf * lax.rsqrt(jnp.mean(xf * xf, axis=-1, keepdims=True) + EPS)
    return (y * g.astype(jnp.float32)).astype(x.dtype)

def rotary(x, positions):
    half = HEAD_DIM // 2
    inv_freq = ROPE_THETA ** (-jnp.arange(half, dtype=jnp.float32) * 2.0 / HEAD_DIM)
    ang = positions.astype(jnp.float32)[..., None] * inv_freq
    cos = jnp.cos(ang)[:, :, None, :]
    sin = jnp.sin(ang)[:, :, None, :]
    xf = x.astype(jnp.float32)
    x1, x2 = xf[..., :half], xf[..., half:]
    return jnp.concatenate([x1 * cos - x2 * sin, x2 * cos + x1 * sin], axis=-1).astype(x.dtype)

def fox_attention(q, k, v, log_f):
    B, S, H, Dh = q.shape
    nb = S // Q_BLOCK
    c = jnp.cumsum(log_f, axis=1)
    c_k = jnp.transpose(c, (0, 2, 1))
    q_blocks = q.reshape(B, nb, Q_BLOCK, H, Dh).transpose(1, 0, 2, 3, 4)
    c_blocks = c.reshape(B, nb, Q_BLOCK, H).transpose(1, 0, 3, 2)
    key_pos = jnp.arange(S)
    scale = HEAD_DIM ** -0.5

    def one_block(args):
        qb, cb, i = args
        s = jnp.einsum('bqhd,bkhd->bhqk', qb, k).astype(jnp.float32) * scale
        s = s + cb[..., None] - c_k[:, :, None, :]
        q_pos = i * Q_BLOCK + jnp.arange(Q_BLOCK)
        causal = key_pos[None, :] <= q_pos[:, None]
        p = jax.nn.softmax(jnp.where(causal, s, -jnp.inf), axis=-1)
        return jnp.einsum('bhqk,bkhd->bqhd', p.astype(v.dtype), v)

    o = lax.map(one_block, (q_blocks, c_blocks, jnp.arange(nb)))
    return o.transpose(1, 0, 2, 3, 4).reshape(B, S, H * Dh)

def swa_sink_attention(q, k, v, sinks):
    B, S, _, Dh = q.shape
    nb = S // WINDOW
    qb = q.reshape(B, nb, WINDOW, SWA_KV_HEADS, SWA_GROUP, Dh)

    def with_prev(t):
        t = t.reshape(B, nb, WINDOW, SWA_KV_HEADS, Dh)
        prev = jnp.pad(t[:, :-1], ((0, 0), (1, 0), (0, 0), (0, 0), (0, 0)))
        return jnp.concatenate([prev, t], axis=2)

    kw, vw = with_prev(k), with_prev(v)
    s = jnp.einsum('bnqhgd,bnkhd->bnhgqk', qb, kw).astype(jnp.float32) * (HEAD_DIM ** -0.5)
    i = jnp.arange(WINDOW)[:, None]
    j = jnp.arange(2 * WINDOW)[None, :]
    dist = WINDOW + i - j
    band = (dist >= 0) & (dist < WINDOW)
    valid = jnp.where((jnp.arange(nb) == 0)[:, None, None], band & (j >= WINDOW), band)
    s = jnp.where(valid[None, :, None, None], s, -jnp.inf)
    sink = jnp.broadcast_to(
        sinks.astype(jnp.float32).reshape(SWA_KV_HEADS, SWA_GROUP)[None, None, :, :, None, None],
        s.shape[:-1] + (1,))
    p = jax.nn.softmax(jnp.concatenate([s, sink], axis=-1), axis=-1)[..., :-1]
    o = jnp.einsum('bnhgqk,bnkhd->bnqhgd', p.astype(v.dtype), vw)
    return o.reshape(B, S, SWA_HEADS * Dh)

def hybrid_mixer(h, positions, w_in, b_forget, b_gate, sinks, w_proj_fox, w_proj_swa, w_out):
    B, S, _ = h.shape
    proj = h @ w_in
    q_f, k_f, v_f, f_logit, q_s, k_s, v_s, gl_f, gl_s = jnp.split(proj, SPLIT_POINTS, axis=-1)
    heads = lambda t, n: t.reshape(B, S, n, HEAD_DIM)
    log_f = jax.nn.log_sigmoid(f_logit.astype(jnp.float32) + b_forget.astype(jnp.float32))
    o_f = fox_attention(heads(q_f, FOX_HEADS), heads(k_f, FOX_HEADS), heads(v_f, FOX_HEADS), log_f)
    o_s = swa_sink_attention(rotary(heads(q_s, SWA_HEADS), positions),
                             rotary(heads(k_s, SWA_KV_HEADS), positions),
                             heads(v_s, SWA_KV_HEADS), sinks)
    g_f = jax.nn.sigmoid(gl_f + b_gate[0])
    g_s = jax.nn.sigmoid(gl_s + b_gate[1])
    merged = g_f * (o_f @ w_proj_fox) + g_s * (o_s @ w_proj_swa)
    return merged @ w_out

def hier_moe(h, w_group, b_group, w_expert, b_expert, w1, w3, w2):
    B, S, D = h.shape
    T = B * S
    hf = h.reshape(T, D)
    g_prob = jax.nn.softmax((hf @ w_group).astype(jnp.float32) + b_group.astype(jnp.float32), axis=-1)
    g_w, g_idx = lax.top_k(g_prob, 1)
    e_logits = ((hf @ w_expert).astype(jnp.float32) + b_expert.astype(jnp.float32)
                ).reshape(T, N_GROUPS, EXPERTS_PER_GROUP)
    e_sel = e_logits[jnp.arange(T), g_idx[:, 0]]
    top_v, top_i = lax.top_k(e_sel, TOP_K)
    gate = (g_w * jax.nn.softmax(top_v, axis=-1)).reshape(-1)
    expert_id = (g_idx * EXPERTS_PER_GROUP + top_i).reshape(-1)
    token_id = jnp.repeat(jnp.arange(T, dtype=jnp.int32), TOP_K)
    A = T * TOP_K
    order = jnp.argsort(expert_id)
    e_sorted = expert_id[order]
    counts = jnp.bincount(expert_id, length=N_EXPERTS)
    padded = (counts + MOE_BLOCK - 1) // MOE_BLOCK * MOE_BLOCK
    start = jnp.cumsum(counts) - counts
    pad_end = jnp.cumsum(padded)
    pad_start = pad_end - padded
    dest = pad_start[e_sorted] + jnp.arange(A) - start[e_sorted]
    P = A + N_EXPERTS * MOE_BLOCK
    n_blk = P // MOE_BLOCK
    row_token = jnp.full((P,), T, jnp.int32).at[dest].set(token_id[order])
    row_gate = jnp.zeros((P,), jnp.float32).at[dest].set(gate[order])
    blk_expert = jnp.minimum(jnp.searchsorted(pad_end, jnp.arange(n_blk) * MOE_BLOCK, side='right'),
                             N_EXPERTS - 1)
    h_pad = jnp.concatenate([hf, jnp.zeros((1, D), hf.dtype)], axis=0)
    xs = h_pad[row_token].reshape(n_blk, MOE_BLOCK, D)

    def expert_block(args):
        xb, e = args
        return (jax.nn.silu(xb @ w1[e]) * (xb @ w3[e])) @ w2[e]

    ys = lax.map(expert_block, (xs, blk_expert)).reshape(P, D)
    out = jnp.zeros((T + 1, D), jnp.float32).at[row_token].add(row_gate[:, None] * ys.astype(jnp.float32))
    return out[:T].reshape(B, S, D).astype(h.dtype)

def first_inputs(seed: int = 0) -> dict:
    key = jax.random.key(seed)
    ks = jax.random.split(key, 20)
    L, D = DEPTH, D_MODEL
    nrm = lambda k, shape, fan_in: jax.random.normal(k, shape, jnp.float32) * fan_in ** -0.5
    return {
        "x": jax.random.normal(ks[0], (BATCH, SEQ, D), jnp.float32),
        "positions": (jnp.arange(SEQ, dtype=jnp.int32)[None, :]
                      + jax.random.randint(ks[1], (BATCH, 1), 0, 1024, jnp.int32)),
        "attn_norm": 1.0 + 0.1 * jax.random.normal(ks[2], (L, D), jnp.float32),
        "w_in": nrm(ks[3], (L, D, N_IN), D),
        "b_forget": jax.random.uniform(ks[4], (L, FOX_HEADS), jnp.float32, 1.0, 4.0),
        "b_gate": 0.02 * jax.random.normal(ks[5], (L, 2, D), jnp.float32),
        "attn_sinks": jax.random.normal(ks[6], (L, SWA_HEADS), jnp.float32),
        "w_proj_fox": nrm(ks[7], (L, FOX_W, D), FOX_W),
        "w_proj_swa": nrm(ks[8], (L, SWA_W, D), SWA_W),
        "w_out": nrm(ks[9], (L, D, D), D),
        "ffn_norm": 1.0 + 0.1 * jax.random.normal(ks[10], (L, D), jnp.float32),
        "w_group": nrm(ks[11], (L, D, N_GROUPS), D),
        "b_group": 0.01 * jax.random.normal(ks[12], (L, N_GROUPS), jnp.float32),
        "w_expert": nrm(ks[13], (L, D, N_EXPERTS), D),
        "b_expert": 0.01 * jax.random.normal(ks[14], (L, N_EXPERTS), jnp.float32),
        "w1": nrm(ks[15], (L, N_EXPERTS, D, D_EXPERT), D),
        "w3": nrm(ks[16], (L, N_EXPERTS, D, D_EXPERT), D),
        "w2": nrm(ks[17], (L, N_EXPERTS, D_EXPERT, D), D_EXPERT),
        "final_norm": 1.0 + 0.1 * jax.random.normal(ks[18], (D,), jnp.float32),
    }

def first_block(x, positions, attn_norm, w_in, b_forget, b_gate, attn_sinks, w_proj_fox, w_proj_swa,
              w_out, ffn_norm, w_group, b_group, w_expert, b_expert, w1, w3, w2, final_norm):
    for l in range(DEPTH):
        h = rms_norm(x, attn_norm[l])
        x = x + hybrid_mixer(h, positions, w_in[l], b_forget[l], b_gate[l], attn_sinks[l],
                             w_proj_fox[l], w_proj_swa[l], w_out[l])
        h = rms_norm(x, ffn_norm[l])
        x = x + hier_moe(h, w_group[l], b_group[l], w_expert[l], b_expert[l], w1[l], w3[l], w2[l])
    return rms_norm(x, final_norm)


PLE_DIM = 256
D_MIX = D_MODEL
RET_HEADS = 4
RET_HEAD_DIM = 128
RET_WIDTH = RET_HEADS * RET_HEAD_DIM
RET_CHUNK = 128
MLA_HEADS = 8
MLA_NOPE_DIM = 64
MLA_ROPE_DIM = 32
MLA_QK_DIM = MLA_NOPE_DIM + MLA_ROPE_DIM
MLA_V_DIM = 64
MLA_WIDTH = MLA_HEADS * MLA_V_DIM
MLA_Q_LORA = 384
MLA_KV_LORA = 256
IN_COLS = 4 * RET_WIDTH + MLA_Q_LORA + MLA_KV_LORA + MLA_ROPE_DIM
D_FF = ((8 * D_MODEL // 3 + 255) // 256) * 256
ROPE_BASE = 10000.0


def rmsnorm(x, w):
    xf = x.astype(jnp.float32)
    y = xf * lax.rsqrt(jnp.mean(xf * xf, axis=-1, keepdims=True) + EPS)
    return (y * w.astype(jnp.float32)).astype(x.dtype)

def head_groupnorm(x, w):
    xf = x.astype(jnp.float32)
    mu = jnp.mean(xf, axis=-1, keepdims=True)
    var = jnp.mean(jnp.square(xf - mu), axis=-1, keepdims=True)
    y = (xf - mu) * lax.rsqrt(var + EPS)
    B, S, H, d = x.shape
    return (y.reshape(B, S, H * d) * w.astype(jnp.float32)).astype(x.dtype)

def rope(x, positions):
    d = x.shape[-1]
    half = d // 2
    inv = 1.0 / (ROPE_BASE ** (jnp.arange(half, dtype=jnp.float32) / half))
    ang = positions.astype(jnp.float32)[..., None] * inv
    cos = jnp.cos(ang)[:, :, None, :].astype(x.dtype)
    sin = jnp.sin(ang)[:, :, None, :].astype(x.dtype)
    x1, x2 = x[..., :half], x[..., half:]
    return jnp.concatenate([x1 * cos - x2 * sin, x2 * cos + x1 * sin], axis=-1)

def retention_chunkwise(q, k, v):
    B, S, H, d = q.shape
    C = RET_CHUNK
    N = S // C
    dt = q.dtype
    log_g = jnp.log(1.0 - 2.0 ** (-5.0 - jnp.arange(H, dtype=jnp.float32)))
    j = jnp.arange(C, dtype=jnp.float32)
    diff = j[:, None] - j[None, :]
    D = jnp.where(diff[None] >= 0, jnp.exp(jnp.maximum(diff, 0.0)[None] * log_g[:, None, None]), 0.0).astype(dt)
    zeta = jnp.exp((C - 1 - j)[None, :] * log_g[:, None]).astype(dt)
    xi = jnp.exp((j + 1)[None, :] * log_g[:, None]).astype(dt)
    g_chunk = jnp.exp(C * log_g).astype(dt)

    qc = q.reshape(B, N, C, H, d)
    kc = k.reshape(B, N, C, H, d)
    vc = v.reshape(B, N, C, H, d)
    scores = jnp.einsum('bnchd,bnmhd->bnhcm', qc, kc) * D[None, None]
    inner = jnp.einsum('bnhcm,bnmhe->bnche', scores, vc)
    U = jnp.einsum('bnmhd,bnmhe,hm->nbhde', kc, vc, zeta)

    def step(R, u):
        return g_chunk[None, :, None, None] * R + u, R

    _, R_prev = lax.scan(step, jnp.zeros_like(U[0]), U)
    cross = jnp.einsum('bnchd,nbhde->bnche', qc, R_prev) * xi.T[None, None, :, :, None]
    return (inner + cross).reshape(B, S, H, d)

def mla_causal(q, k, v):
    B, S, H, dqk = q.shape
    dv = v.shape[-1]
    NB = S // Q_BLOCK
    scale = 1.0 / math.sqrt(dqk)
    kt = k.transpose(0, 2, 1, 3)
    vt = v.transpose(0, 2, 1, 3)
    qb = q.reshape(B, NB, Q_BLOCK, H, dqk).transpose(1, 0, 3, 2, 4)
    kpos = jnp.arange(S)

    def block(args):
        qi, bi = args
        s = jnp.einsum('bhqd,bhkd->bhqk', qi, kt).astype(jnp.float32) * scale
        qpos = bi * Q_BLOCK + jnp.arange(Q_BLOCK)
        mask = kpos[None, :] <= qpos[:, None]
        s = jnp.where(mask[None, None], s, -1e30)
        pr = jax.nn.softmax(s, axis=-1).astype(vt.dtype)
        return jnp.einsum('bhqk,bhkd->bhqd', pr, vt)

    out = lax.map(block, (qb, jnp.arange(NB)))
    return out.transpose(1, 0, 3, 2, 4).reshape(B, S, H * dv)

def token_mixer(xn, positions, w_in, ret_gn_w, mla_q_norm, w_uq, mla_kv_norm, w_ukv, w_o):
    B, S, _ = xn.shape
    proj = xn @ w_in
    o = 0
    rq = proj[..., o:o + RET_WIDTH]; o += RET_WIDTH
    rk = proj[..., o:o + RET_WIDTH]; o += RET_WIDTH
    rv = proj[..., o:o + RET_WIDTH]; o += RET_WIDTH
    rg = proj[..., o:o + RET_WIDTH]; o += RET_WIDTH
    cq = proj[..., o:o + MLA_Q_LORA]; o += MLA_Q_LORA
    ckv = proj[..., o:o + MLA_KV_LORA]; o += MLA_KV_LORA
    kr = proj[..., o:o + MLA_ROPE_DIM]

    shp = (B, S, RET_HEADS, RET_HEAD_DIM)
    rq = rope(rq.reshape(shp), positions)
    rk = rope(rk.reshape(shp), positions) * (RET_HEAD_DIM ** -0.5)
    ry = retention_chunkwise(rq, rk, rv.reshape(shp))
    ret_out = jax.nn.silu(rg) * head_groupnorm(ry, ret_gn_w)

    qh = (rmsnorm(cq, mla_q_norm) @ w_uq).reshape(B, S, MLA_HEADS, MLA_QK_DIM)
    q = jnp.concatenate([qh[..., :MLA_NOPE_DIM], rope(qh[..., MLA_NOPE_DIM:], positions)], axis=-1)
    kvh = (rmsnorm(ckv, mla_kv_norm) @ w_ukv).reshape(B, S, MLA_HEADS, MLA_NOPE_DIM + MLA_V_DIM)
    k_rope = rope(kr[:, :, None, :], positions)
    k = jnp.concatenate([kvh[..., :MLA_NOPE_DIM],
                         jnp.broadcast_to(k_rope, (B, S, MLA_HEADS, MLA_ROPE_DIM))], axis=-1)
    v = kvh[..., MLA_NOPE_DIM:]
    mla_out = mla_causal(q, k, v)

    return jnp.concatenate([ret_out, mla_out], axis=-1) @ w_o

def second_inputs(seed: int = 0) -> dict:
    key = jax.random.key(seed)
    ks = jax.random.split(key, 24)
    L = DEPTH

    def nrm(k, shape, fan_in):
        return jax.random.normal(k, shape, jnp.float32) * (fan_in ** -0.5)

    def gain(k, shape):
        return 1.0 + 0.05 * jax.random.normal(k, shape, jnp.float32)

    return {
        "x": jax.random.normal(ks[0], (BATCH, SEQ, D_MODEL), jnp.float32),
        "p": jax.random.normal(ks[1], (DEPTH, BATCH, SEQ, PLE_DIM), jnp.float32),
        "positions": jnp.broadcast_to(jnp.arange(SEQ, dtype=jnp.int32)[None], (BATCH, SEQ)),
        "pre_mix_norm": gain(ks[2], (L, D_MODEL)),
        "w_in": nrm(ks[3], (L, D_MODEL, IN_COLS), D_MODEL),
        "ret_gn_w": gain(ks[4], (L, RET_WIDTH)),
        "mla_q_norm": gain(ks[5], (L, MLA_Q_LORA)),
        "w_uq": nrm(ks[6], (L, MLA_Q_LORA, MLA_HEADS * MLA_QK_DIM), MLA_Q_LORA),
        "mla_kv_norm": gain(ks[7], (L, MLA_KV_LORA)),
        "w_ukv": nrm(ks[8], (L, MLA_KV_LORA, MLA_HEADS * (MLA_NOPE_DIM + MLA_V_DIM)), MLA_KV_LORA),
        "w_o": nrm(ks[9], (L, D_MIX, D_MODEL), D_MIX),
        "post_mix_norm": gain(ks[10], (L, D_MODEL)),
        "pre_ffn_norm": gain(ks[11], (L, D_MODEL)),
        "w_gate": nrm(ks[12], (L, D_MODEL, D_FF), D_MODEL),
        "w_up": nrm(ks[13], (L, D_MODEL, D_FF), D_MODEL),
        "w_down": nrm(ks[14], (L, D_FF, D_MODEL), D_FF),
        "post_ffn_norm": gain(ks[15], (L, D_MODEL)),
        "w_ple_proj": nrm(ks[16], (L, PLE_DIM, D_MODEL), PLE_DIM),
        "ple_norm": gain(ks[17], (L, D_MODEL)),
        "w_ple_gate": nrm(ks[18], (L, D_MODEL, D_MODEL), D_MODEL),
        "b_ple_gate": 0.02 * jax.random.normal(ks[19], (L, D_MODEL), jnp.float32),
    }

def second_block(x, p, positions, pre_mix_norm, w_in, ret_gn_w, mla_q_norm, w_uq, mla_kv_norm,
              w_ukv, w_o, post_mix_norm, pre_ffn_norm, w_gate, w_up, w_down, post_ffn_norm,
              w_ple_proj, ple_norm, w_ple_gate, b_ple_gate):
    h = x
    for i in range(DEPTH):
        xn = rmsnorm(h, pre_mix_norm[i])
        mix = token_mixer(xn, positions, w_in[i], ret_gn_w[i], mla_q_norm[i], w_uq[i],
                          mla_kv_norm[i], w_ukv[i], w_o[i])
        h = h + rmsnorm(mix, post_mix_norm[i])
        hn = rmsnorm(h, pre_ffn_norm[i])
        ff = (jax.nn.silu(hn @ w_gate[i]) * (hn @ w_up[i])) @ w_down[i]
        h = h + rmsnorm(ff, post_ffn_norm[i])
        e = rmsnorm(p[i] @ w_ple_proj[i], ple_norm[i])
        gate = jax.nn.sigmoid(h @ w_ple_gate[i] + b_ple_gate[i])
        h = h + e * gate
    return h


def setup_inputs(seed=0):
    out = dict(first_inputs(seed))
    for name, value in second_inputs(seed + 1).items():
        if name != "x":
            out[name + "_2"] = value
    return out


def reference(
    x, positions, attn_norm, w_in, b_forget, b_gate, attn_sinks, w_proj_fox, w_proj_swa, w_out,
    ffn_norm, w_group, b_group, w_expert, b_expert, w1, w3, w2, final_norm, p_2, positions_2,
    pre_mix_norm_2, w_in_2, ret_gn_w_2, mla_q_norm_2, w_uq_2, mla_kv_norm_2, w_ukv_2, w_o_2,
    post_mix_norm_2, pre_ffn_norm_2, w_gate_2, w_up_2, w_down_2, post_ffn_norm_2, w_ple_proj_2,
    ple_norm_2, w_ple_gate_2, b_ple_gate_2,
):
    x = first_block(
        x, positions, attn_norm, w_in, b_forget, b_gate, attn_sinks, w_proj_fox, w_proj_swa,
        w_out, ffn_norm, w_group, b_group, w_expert, b_expert, w1, w3, w2, final_norm,
    )
    return second_block(
        x, p_2, positions_2, pre_mix_norm_2, w_in_2, ret_gn_w_2, mla_q_norm_2, w_uq_2,
        mla_kv_norm_2, w_ukv_2, w_o_2, post_mix_norm_2, pre_ffn_norm_2, w_gate_2, w_up_2,
        w_down_2, post_ffn_norm_2, w_ple_proj_2, ple_norm_2, w_ple_gate_2, b_ple_gate_2,
    )


_drawn_inputs = setup_inputs


def setup_inputs(seed=0):
    import zlib

    import numpy as np

    out = dict(_drawn_inputs(seed))
    spreads = {}
    factors = {'b_gate': 3.277,
     'b_group': 2.67,
     'b_expert': 2.875,
     'mla_q_norm_2': 6.583,
     'mla_kv_norm_2': 4.233,
     'ple_norm_2': 3.594,
     'b_ple_gate_2': 8.0,
     'ret_gn_w_2': 8.0}
    for name, (base, spread) in spreads.items():
        noise = np.random.default_rng([zlib.crc32(name.encode()), seed]).standard_normal(out[name].shape)
        drawn = base * np.exp(spread * noise) if base else spread * noise
        out[name] = __import__('jax').numpy.asarray(drawn.astype(out[name].dtype))
    for name, factor in factors.items():
        out[name] = (out[name] * factor).astype(out[name].dtype)
    return out
```

```python
from contextlib import ExitStack

import numpy as np

import concourse.bass as bass
from concourse import mybir

F32 = mybir.dt.float32
F32R = mybir.dt.float32r
I32 = mybir.dt.int32
U32 = mybir.dt.uint32
ALU = mybir.AluOpType
ACT = mybir.ActivationFunctionType
AX = mybir.AxisListType

P = 128
T = 512
NT = T // P
D = 1024
DC = D // P
EPS = 1e-6
HD, H1, KVH, GRP = 64, 8, 2, 4
W1 = H1 * HD
W1C = W1 // P
NG, EG, NE, DE = 8, 8, 64, 512
NR = NG + NE
CF, CQS, CKS, CGF, CGS = 3 * W1, 3 * W1 + H1, 4 * W1 + H1, 4 * W1 + H1 + 2 * KVH * HD, 4 * W1 + H1 + 2 * KVH * HD + D
RH, RD = 4, 128
QL, KVL, ML_H, ML_N, ML_R, ML_V = 384, 256, 8, 64, 32, 64
ML_QK = ML_N + ML_R
DFF = 2816
FC = DFF // P
PLE = 256
BLK = 32
EB = T // BLK
SPILL = 2 * T // BLK
NBLK = NE + SPILL
NOTHING = 1 << 16
BIG = 1.0e30
UNIT = 2048
RAW, PARTS = 3, 2
HALVES = 6

CONST_COLS = {}


def constants():
    parts, at = [], 0

    def put(name, a):
        nonlocal at
        full = np.zeros((P, a.shape[1]), np.float32)
        full[:a.shape[0]] = a
        CONST_COLS[name] = (at, at + a.shape[1])
        at += a.shape[1]
        parts.append(full)

    p = np.arange(P)[:, None]
    c = np.arange(P)[None, :]

    def rotation(width, half):
        m = np.zeros((P, P), np.float32)
        for g in range(0, width, 2 * half):
            for j in range(half):
                m[g + half + j, g + j] = -1.0
                m[g + j, g + half + j] = 1.0
        return m

    put("ident", np.eye(P, dtype=np.float32))
    put("rot_swa", rotation(P, HD // 2))
    put("rot_ret", rotation(P, RD // 2))
    rot_mla = np.zeros((P, P), np.float32)
    for j in range(ML_R // 2):
        rot_mla[ML_N + ML_R // 2 + j, ML_N + j] = -1.0
        rot_mla[ML_N + j, ML_N + ML_R // 2 + j] = 1.0
    put("rot_mla", rot_mla)
    put("causal", np.concatenate([np.zeros((P, T - P)), np.where(c > p, BIG, 0.0)], 1))
    put("window", np.concatenate([np.where(c > p, 0.0, BIG), np.where(c > p, BIG, 0.0)], 1))
    put("upto", (np.arange(T)[None, :] >= p).astype(np.float32))
    put("before", (c > p).astype(np.float32))
    put("ones", np.ones((P, P)))
    f = 10000.0
    put("inv_swa", (f ** (-(p % 32).astype(np.float32) * np.float32(2.0) / np.float32(64))).astype(np.float32))
    put("inv_ret", (1.0 / (f ** ((p % 64).astype(np.float32) / np.float32(64)))).astype(np.float32))
    mla = (1.0 / (f ** ((p % 16).astype(np.float32) / np.float32(16)))).astype(np.float32)
    put("inv_mla", np.where((p >= ML_N) & (p < ML_QK), mla, 0.0))
    put("id2", np.concatenate([2.0 * (p + P * np.arange(NT)[None, :]) + k for k in range(2)], 1))
    return np.concatenate(parts, 1).astype(np.float32)


def late_constants():
    p = np.arange(P)[:, None]
    d = np.arange(T)[None, :] - p
    out = []
    for h in range(RH):
        lg = np.log(1.0 - 2.0 ** (-5.0 - h))
        out.append(np.where(d >= 0, np.exp(np.maximum(d, 0) * lg), 0.0))
    return np.concatenate(out, 1).astype(np.float32)


def route_constants():
    a = np.zeros((P, 128), np.float32)
    a[:, 0:NE] = np.arange(NE)
    a[:, NE:NE + NG] = np.arange(NG)
    a[:, 72:72 + EB - 1] = BLK * np.arange(1, EB)
    a[:, 96] = EB * np.arange(P) + 1
    return a


PARAM_COLS = {}


def params(inputs):
    parts, at = [], 0
    for name, a in [("attn_norm", inputs["attn_norm"]), ("b_gate", inputs["b_gate"]),
                    ("pre_mix", inputs["pre_mix_norm_2"]), ("pre_ffn", inputs["pre_ffn_norm_2"]),
                    ("mla_q", inputs["mla_q_norm_2"]), ("mla_kv", inputs["mla_kv_norm_2"]),
                    ("ret_gn", inputs["ret_gn_w_2"])]:
        a = np.asarray(a).reshape(-1, P).T
        PARAM_COLS[name] = (at, at + a.shape[1])
        at += a.shape[1]
        parts.append(a)
    return np.ascontiguousarray(np.concatenate(parts, 1))


class Job:

    def __init__(self, bank, use):
        self.bank, self.use = bank, use


class Banks:

    def __init__(self):
        self.uses, self.next = [0] * 8, 0

    def take(self, n, among=None):
        jobs = []
        for i in range(n):
            if among is None:
                b = self.next
                self.next = (self.next + 1) % 8
            else:
                b = among[i % len(among)]
            jobs.append(Job(b, self.uses[b]))
            self.uses[b] += 1
        return jobs


class Unit:

    def __init__(self, n, src, chunks, cols, copies):
        self.n, self.src, self.chunks, self.cols, self.copies = n, src, chunks, cols, copies
        self.last, self.part = None, None


def build(nc, a, out, stop=99):
    ctx = ExitStack()
    with ctx:
        def sb(name, shape, dt=F32):
            return ctx.enter_context(nc.sbuf_tensor(name, shape, dt))

        def sem(name):
            return ctx.enter_context(nc.semaphore(name))

        base = -(-nc.sbuf_base // 32) * 32

        def at(name, lo, shape, dt=F32):
            return nc.alloc_sbuf_tensor_at(name, [P] + shape, dt, offset=base + 4 * lo)

        x = at("x", 0, [NT, D])
        n_cst, n_prm = -(-a["consts"].shape[1] // 8) * 8, -(-a["params"].shape[1] // 8) * 8
        cst = at("cst", 4096, [a["consts"].shape[1]])
        prm = at("prm", 4096 + n_cst, [a["params"].shape[1]])
        small = at("small", 4096 + n_cst + n_prm, [512])
        lo = 4096 + n_cst + n_prm + 512
        F0 = lo
        W0 = F0 + 31984
        scratch = at("scratch", F0, [4096])
        ofTh, ofTl = at("ofTh", F0 + 4096, [4, T], F32R), at("ofTl", F0 + 6144, [4, T], F32R)
        side = at("side", F0 + 4096, [4096])
        hTh, hTl = at("hTh", F0 + 8192, [DC, T], F32R), at("hTl", F0 + 12288, [DC, T], F32R)
        rows = at("rows", F0 + 8192, [4, D])
        ffo = at("ffo", F0 + 12288, [NT, D])
        arena = at("arena", F0 + 16384, [12288])
        osTh, osTl = at("osTh", F0 + 16384, [4, T], F32R), at("osTl", F0 + 18432, [4, T], F32R)
        o_tok = at("o_tok", F0 + 28672, [NT, T])
        ffh = at("ffh", F0 + 16384, [FC, T], F32R)
        ffl0 = at("ffl0", F0 + 27648, [8, T], F32R)
        ffl1 = at("ffl1", F0 + 1024, [FC - 8, T], F32R)
        wf_h, wf_l = [at(n, F0 + 16384 + 11392 + 64 * k, [DC, H1], F32R) for k, n in enumerate(("wf_h", "wf_l"))]
        raw = at("raw", W0, [RAW, UNIT])
        w_hi = at("w_hi", W0 + RAW * UNIT, [PARTS, UNIT], F32R)
        w_lo = at("w_lo", W0 + (RAW + PARTS) * UNIT, [PARTS, UNIT], F32R)
        m_xh, m_xl = at("m_xh", F0 + 4096, [DC, BLK], F32R), at("m_xl", F0 + 4352, [DC, BLK], F32R)
        m_ah, m_al = at("m_ah", F0 + 4608, [4, BLK], F32R), at("m_al", F0 + 4736, [4, BLK], F32R)
        m_whi = at("m_whi", W0 - 2 * HALVES * UNIT, [HALVES, UNIT], F32R)
        m_wlo = at("m_wlo", W0 - HALVES * UNIT, [HALVES, UNIT], F32R)
        m_raw = at("m_raw", W0, [HALVES, UNIT])
        bf_row = small[:, 0:8]
        sink_row = small[:, 8:16]
        nsink = small[:, 16:24]
        ssq = small[:, 24:28]
        rstd = small[:, 28:32]
        ssq2 = small[:, 32:36]
        rstd2 = small[:, 36:40]
        negm = small[:, 40:104]
        psums = small[:, 104:168]
        precip = small[:, 168:232]
        psink = small[:, 232:296]
        gates = small[:, 296:304].rearrange("p (i k) -> p i k", k=2)
        route = small[:, 304:512]

        def C(name):
            lo, hi = CONST_COLS[name]
            return cst[:, lo:hi]

        def PRM(name, i=0):
            lo, _ = PARAM_COLS[name]
            return prm[:, lo + i:lo + i + 1]

        ident = C("ident")
        banks = [ctx.enter_context(nc.psum_tensor(f"bank{b}", [P, 512], F32)) for b in range(8)]
        h_rows = nc.dram_tensor("h_rows", (T, D), F32, kind="Internal").ap()
        y_rows = nc.dram_tensor("y_rows", (2 * T, D), F32, kind="Internal").ap()
        slot_ids = nc.dram_tensor("slot_ids", (NE * T, 1), I32, kind="Internal").ap()

        filled = [sem(f"filled{b}") for b in range(8)]
        freed = [sem(f"freed{b}") for b in range(8)]
        arrived = [sem(f"arrived{s}") for s in range(RAW)]
        hi_made, lo_made = sem("hi_made"), sem("lo_made")
        split_hi = sem("split_hi")

        def claim(pe, job):
            if job.use:
                pe.wait_ge(freed[job.bank], job.use)

        def full(eng, job):
            eng.wait_ge(filled[job.bank], job.use + 1)

        def read(eng, jobs):
            last = {}
            for j in jobs:
                last[j.bank] = max(last.get(j.bank, 0), j.use + 1)
            for b, n in last.items():
                eng.wait_ge(freed[b], n)

        def fill(ins, job):
            ins.then_inc(filled[job.bank], 1)

        def free(ins, job):
            ins.then_inc(freed[job.bank], 1)

        class Chain:

            def __init__(self, eng, s):
                self.eng, self.s, self.n = eng, s, 0

            def __call__(self, ins):
                self.n += 1
                ins.then_inc(self.s, 1)
                self.eng.wait_ge(self.s, self.n)

        units_of, order = {}, []

        def unit(name, src, chunks, cols, copies=1):
            u = Unit(len(order), src, chunks, cols, copies)
            order.append(u)
            u.loads = 16 * sum(w.copies for w in order[u.n % RAW::RAW])
            units_of.setdefault(name, []).append(u)

        def cols_of(w, lo, hi):
            return w[:, lo:hi].rearrange("(c p) n -> p c n", p=P)

        def stationary(name, w, lo, n, step=256):
            for c in range(lo, lo + n, step):
                k = min(step, lo + n - c)
                unit(name, cols_of(w, c, c + k), w.shape[0] // P, k)

        def moving(name, w, lo, n, step=512):
            step = min(step, w.shape[0])
            for r in range(0, w.shape[0], step):
                k = min(step, w.shape[0] - r)
                unit(name, cols_of(w[r:r + k, :], lo, lo + n), k // P, n)

        win, win2 = a["w_in"][0], a["w_in_2"][0]
        stationary("qs", win, CQS, W1)
        for g in range(KVH):
            unit("ks", cols_of(win, CKS + HD * g, CKS + HD * (g + 1)), DC, 2 * HD, 2)
        stationary("qf", win, 0, W1)
        stationary("kf", win, W1, W1)
        stationary("vs", win, CKS + KVH * HD, KVH * HD)
        moving("vf", win, 2 * W1, W1)
        stationary("gf", win, CGF, D)
        stationary("gs", win, CGS, D)
        stationary("pf", a["w_proj_fox"][0], 0, D, 512)
        stationary("ps", a["w_proj_swa"][0], 0, D, 512)
        for n in range(2):
            moving(f"out{n}", a["w_out"][0], 512 * n, 512)
        n_first = len(order)
        stationary("rq", win2, 0, 512)
        stationary("rk", win2, 512, 512)
        moving("rv", win2, 1024, 512)
        stationary("rg", win2, 1536, 512)
        moving("lat0", win2, 2048, 512)
        stationary("lat1", win2, 2560, 160)
        stationary("uq", a["w_uq_2"][0], 0, ML_H * ML_QK, ML_H * ML_QK // 2)
        stationary("ukv", a["w_ukv_2"][0], 0, ML_H * (ML_N + ML_V), 1024)
        for n in range(2):
            moving(f"o{n}", a["w_o_2"][0], 512 * n, 512)
        n_ff = DFF // 256
        for n in range(n_ff):
            stationary("gate", a["w_gate_2"][0], 256 * n, 256)
            stationary("up", a["w_up_2"][0], 256 * n, 256)
        moving("down", a["w_down_2"][0], 0, D, 256)
        moving("ple", a["w_ple_proj_2"][0], 0, D, 256)
        for n in range(2):
            moving(f"pg{n}", a["w_ple_gate_2"][0], 512 * n, 512)
        n_part = [0]

        def parts(u):
            shape = "p (c n) -> p c n"
            n = u.chunks * u.cols
            return (w_hi[:, u.n % PARTS, 0:n].rearrange(shape, c=u.chunks),
                    w_lo[:, u.n % PARTS, 0:n].rearrange(shape, c=u.chunks))

        def loaded(pe, u):
            pe.wait_ge(lo_made, u.n + 1)

        def used(eng, u):
            if u.part is None:
                full(eng, u.last)
            else:
                eng.wait_ge(S("part_used"), u.part)

        bk = Banks()
        J = {}

        def plan(name, n, how=None, among=None):
            J[name] = bk.take(n, among)
            if how:
                us = units_of[name]
                for k, u in enumerate(us):
                    if how == "each":
                        u.last = J[name][(k + 1) * n // len(us) - 1]
                    elif k == len(us) - 1:
                        u.last = J[name][-1]
                    else:
                        n_part[0] += 1
                        u.part = n_part[0]

        plan("hT1", DC)
        plan("zT", 1)
        plan("qs", W1C, "each")
        plan("flog", 1)
        plan("ks", KVH, "each")
        plan("qf", W1C, "each")
        plan("qs_rot", W1C)
        plan("ks_rot", KVH)
        plan("kf", W1C, "each")
        plan("cT", 1)
        plan("vs", NT, "each")
        plan("vf", NT, "sum")
        S_B, T_B, V_B = (0, 1, 2), (3, 4, 5), (6, 7)

        def plan_attention(name, units, extra=0):
            bk.next = 0
            J[name + "_s"] = bk.take(units, S_B)
            J[name + "_t"] = bk.take(units, T_B)
            J[name + "_v"] = bk.take(units, V_B)
            J[name + "_oT"] = bk.take(W1C)

        bk.next = 0
        J["decay"] = []
        plan_attention_units = H1 * NT
        J["fox_s"] = bk.take(plan_attention_units, S_B)
        J["fox_t"] = bk.take(plan_attention_units, T_B)
        J["fox_v"] = []
        vb = 0
        for u in range(plan_attention_units + 3):
            if u < plan_attention_units and u % NT == 0:
                J["decay"] += bk.take(1, (V_B[vb % 2],))
                vb += 1
            if u >= 3:
                J["fox_v"] += bk.take(1, (V_B[vb % 2],))
                vb += 1
        plan_attention("swa", H1 * NT)
        J["fox_oT"] = bk.take(W1C)
        for name in ("gf", "gs", "pf", "ps"):
            plan(name, DC, "each")
        for n in range(2):
            plan(f"out{n}", NT, "sum")
        plan("hT2", DC)
        plan("router", NT)
        plan("rank", NT)
        plan("count", 1)
        plan("starts", 1)
        plan("further", 1)
        plan("ids", 2)
        J["before_moe"] = bk.take(8)
        plan("hT3", DC)
        plan("rq", RH, "each")
        plan("rk", RH, "each")
        plan("rq_rot", RH)
        plan("rk_rot", RH)
        plan("rv", NT, "sum")
        plan("rg", RH, "each")
        plan("lat0", NT, "sum")
        plan("lat1", NT)
        plan("kr", 1)
        units_of["lat1"][0].last = J["kr"][-1]
        J["ret_s"] = bk.take(RH * NT, (0, 1, 2, 3))
        J["ret_v"] = bk.take(RH, (4, 5))
        J["ret_m"] = bk.take(2 * RH, (6, 7))
        bk.next = 0
        plan("cqT", QL // P)
        plan("ckvT", KVL // P)
        plan("kr_rot", 1)
        plan("mq", ML_H)
        for k, u in enumerate(units_of["uq"]):
            u.last = J["mq"][4 * k + 3]
        plan("mq_rot", ML_H)
        plan("mk", ML_H)
        plan("mv", NT)
        units_of["ukv"][0].last = J["mv"][-1]
        plan_attention("mla", ML_H * NT)
        for n in range(2):
            plan(f"o{n}", NT, "sum")
        plan("hT4", DC)
        J["gate"], J["up"] = [], []
        for n in range(n_ff):
            for _ in range(2):
                J["gate"] += bk.take(1)
                J["up"] += bk.take(1)
            units_of["gate"][n].last = J["gate"][-1]
            units_of["up"][n].last = J["up"][-1]
        plan("down", 8, "sum")
        plan("pT", PLE // P)
        plan("ple", 2 * NT, "sum")
        plan("hT5", DC)
        for n in range(2):
            plan(f"pg{n}", NT, "sum")

        def av(lo, n, *dims):
            v = arena[:, lo:lo + n]
            return v.rearrange("p (a b) -> p a b", a=dims[0]) if dims else v

        def xn(i):
            return av(4096 + 1024 * i, 1024)

        qfT, kfT = av(0, 2048, 4), av(2048, 2048, 4)
        vf = av(4096, 2048, NT)
        qsT = av(6144, 2048, 4)
        ksT = av(8192, 1024, 2)
        vs = av(9216, 512, NT)
        Pb = av(9728, 1536, 3)
        PTb = av(11264, 1024, 2)
        cos1, sin1 = scratch[:, 0:512], scratch[:, 512:1024]
        tmp = [scratch[:, 1024 + 512 * k:1536 + 512 * k] for k in range(2)]
        cT = scratch[0:H1, 2048:2560]
        decay_row = [scratch[:, 2560 + 512 * k:3072 + 512 * k] for k in range(2)]
        pos_i = scratch[:, 3584:4096].bitcast(I32)
        ang, red = scratch[:, 2560:3072], scratch[:, 3072:3584]
        posf = scratch[:, 2048:2560]
        w_f = arena[:, 11264:11264 + DC * H1].rearrange("p (c n) -> p c n", c=DC)
        zT = scratch[0:H1, 1536:2048]
        logf = small[:, 304:336].rearrange("p (i h) -> p i h", h=H1)
        logf_t = small[:, 336:368].rearrange("p (i h) -> p i h", h=H1)
        logf_z = small[:, 368:400].rearrange("p (i h) -> p i h", h=H1)
        gfT, gsT = av(4096, 4096, DC), av(8192, 4096, DC)

        def chunks_of(h, l, first=0):
            return (lambda c: h[:, first + c, :]), (lambda c: l[:, first + c, :])

        hT, ofT, osT = chunks_of(hTh, hTl), chunks_of(ofTh, ofTl), chunks_of(osTh, osTl)

        s_const, s_pos, s_wf = sem("s_const"), sem("s_pos"), sem("s_wf")
        s_x = [sem(f"s_x{i}") for i in range(NT)]

        dve_own, act_own, pool_own = sem("dve_own"), sem("act_own"), sem("pool_own")
        NORMS = {name: k + 1 for k, name in enumerate(["n1", "n2", "n3", "n4", "nq", "nk", "n5", "n6", "n7", "n8"])}
        ROPES = {name: k + 1 for k, name in enumerate(["rope1", "rope2", "rope3"])}

        st = {}

        def S(name):
            if name not in st:
                st[name] = sem(name)
            return st[name]

        block = ctx.enter_context(nc.Block())

        def act_sumsq(act, chain, name, src, n, junk, into, before=None):
            for i in range(n):
                if before:
                    before(i)
                chain(act.activation(junk, src(i), ACT.Square, accum_out=into[:, i:i + 1]))
            act.sem_inc(S("norm_squares"), 1)

        def act_sqrt(act, name, r, n):
            act.wait_ge(S("norm_means"), NORMS[name])
            act.activation(r[:, 0:n], r[:, 0:n], ACT.Sqrt).then_inc(S("norm_roots"), 1)

        def dve_rstd(v, chain, name, ss, r, n, width):
            v.wait_ge(S("norm_squares"), NORMS[name])
            v.tensor_scalar(r[:, 0:n], ss[:, 0:n], 1.0 / width, EPS, ALU.mult, ALU.add).then_inc(S("norm_means"), 1)
            v.wait_ge(S("norm_roots"), NORMS[name])
            chain(v.reciprocal(r[:, 0:n], r[:, 0:n]))

        def pe_to_feature(pe, jobs, src, nt=NT):
            for c, job in enumerate(jobs):
                claim(pe, job)
                for i in range(nt):
                    mm = pe.transpose(banks[job.bank][:, P * i:P * (i + 1)], src(i, c), ident)
                fill(mm, job)

        def three(pe, dst, left, right, start, stop):
            pe.matmul(dst, left[0], right[0], start=start, stop=False)
            pe.matmul(dst, left[1], right[0], start=False, stop=False)
            return pe.matmul(dst, left[0], right[1], start=False, stop=stop)

        def pe_feature(pe, name, act_in, step=P, m=P):
            us, jobs = units_of[name], J[name]
            each = len(jobs) // len(us)
            for j, job in enumerate(jobs):
                u, lo = us[j // each], step * (j % each)
                if j % each == 0:
                    loaded(pe, u)
                wh, wl = parts(u)
                claim(pe, job)
                for c in range(u.chunks):
                    mm = three(pe, banks[job.bank][0:m, :], (wh[:, c, lo:lo + m], wl[:, c, lo:lo + m]),
                               (act_in[0](c), act_in[1](c)), c == 0, c == u.chunks - 1)
                fill(mm, job)

        def pe_token(pe, name, act_in, place=None, wait=None):
            us, jobs = units_of[name], J[name]
            c0 = 0
            for k, u in enumerate(us):
                loaded(pe, u)
                if wait:
                    wait(k)
                wh, wl = parts(u)
                last = k == len(us) - 1
                for j, job in enumerate(jobs):
                    i, lo = place(j) if place else (j, 0)
                    if k == 0:
                        claim(pe, job)
                    t = slice(P * i, P * (i + 1))
                    for c in range(u.chunks):
                        mm = three(pe, banks[job.bank][:, :], (act_in[0](c0 + c)[:, t], act_in[1](c0 + c)[:, t]),
                                   (wh[:, c, lo:lo + 512], wl[:, c, lo:lo + 512]), k == 0 and c == 0,
                                   last and c == u.chunks - 1)
                    if last:
                        fill(mm, job)
                if not last:
                    mm.then_inc(S("part_used"), 1)
                c0 += u.chunks

        class Split:

            def __init__(self):
                self.n, self.limit = 0, n_first

        hi_at, lo_at = Split(), Split()

        def hi_until(act, n):
            while hi_at.n <= min(n, hi_at.limit - 1):
                k = hi_at.n
                u = order[k]
                size = u.chunks * u.cols
                act.wait_ge(arrived[k % RAW], u.loads)
                if k >= PARTS:
                    used(act, order[k - PARTS])
                act.activation(w_hi[:, k % PARTS, 0:size], raw[:, k % RAW, 0:size], ACT.Copy).then_inc(hi_made, 1)
                hi_at.n += 1

        def lo_until(v, n):
            while lo_at.n <= min(n, lo_at.limit - 1):
                k = lo_at.n
                size = order[k].chunks * order[k].cols
                v.wait_ge(hi_made, k + 1)
                v.tensor_tensor(w_lo[:, k % PARTS, 0:size], raw[:, k % RAW, 0:size],
                                w_hi[:, k % PARTS, 0:size].bitcast(F32), ALU.subtract).then_inc(lo_made, 1)
                lo_at.n += 1

        def ahead(until, eng, name, j=0):
            us = units_of[name]
            if us[0].part is None:
                until(eng, us[j * len(us) // len(J[name])].n + 1)
            else:
                until(eng, us[-1].n + 1)

        splits = [0]
        hi_number = {}

        def act_split(act, key, dst, src, scale=1.0):
            act.activation(dst, src, ACT.Copy, scale=scale).then_inc(split_hi, 1)
            splits[0] += 1
            hi_number[key] = splits[0]

        def act_split_jobs(act, name, h, scale=None, first=0):
            for c, job in enumerate(J[name]):
                full(act, job)
                act_split(act, (name, c), h[:, first + c, :], banks[job.bank][:, :], scale(c) if scale else 1.0)

        def dve_split(v, key, dst, src, h, scale=None):
            v.wait_ge(split_hi, hi_number[key])
            if scale is None:
                return v.tensor_tensor(dst, src, h.bitcast(F32), ALU.subtract)
            return v.scalar_tensor_tensor(dst, src, scale, h.bitcast(F32), ALU.mult, ALU.subtract)

        def dve_split_jobs(v, name, h, l, scale=None, first=0):
            for c, job in enumerate(J[name]):
                free(dve_split(v, (name, c), l[:, first + c, :], banks[job.bank][:, :], h[:, first + c, :],
                               scale(c) if scale else None), job)

        class Attention:

            def __init__(self, name, units, q, k, v, added, width, keys, outp, sink=False, mask_by_pe=False):
                self.name, self.units = name, units
                self.q, self.k, self.v, self.added = q, k, v, added
                self.width, self.keys, self.outp = width, keys, outp
                self.sink, self.mask_by_pe = sink, mask_by_pe
                self.js, self.jt, self.jv = J[name + "_s"], J[name + "_t"], J[name + "_v"]
                self.P, self.PT = Pb, PTb
                self.base = {"fox": 0, "swa": 1, "mla": 2}[name] * len(units)

        def pe_attention(pe, A, before=None):
            n = len(A.units)
            for t in range(n + 3):
                if t < n:
                    if before:
                        before(t)
                    job = A.js[t]
                    claim(pe, job)
                    w = A.width(t)
                    mm = pe.matmul(banks[job.bank][:, 0:w], A.q(t), A.k(t), start=True, stop=not A.mask_by_pe)
                    if A.mask_by_pe:
                        mm = pe.matmul(banks[job.bank][:, w - P:w], ident, C("causal")[:, T - P:T], start=False, stop=True)
                    fill(mm, job)
                if 0 <= t - 2 < n:
                    u = t - 2
                    job = A.jt[u]
                    claim(pe, job)
                    pe.wait_ge(S("exp"), A.base + u + 1)
                    for b in range(A.width(u) // P):
                        mm = pe.transpose(banks[job.bank][:, P * b:P * (b + 1)], A.P[:, u % 3, P * b:P * (b + 1)], ident)
                    fill(mm, job)
                if 0 <= t - 3:
                    u = t - 3
                    job = A.jv[u]
                    claim(pe, job)
                    read(pe, [A.jt[u]])
                    nb = A.width(u) // P
                    for b in range(nb):
                        mm = pe.matmul(banks[job.bank][:, 0:HD], A.PT[:, u % 2, P * b:P * (b + 1)], A.v(u, b),
                                       start=(b == 0), stop=(b == nb - 1))
                    fill(mm, job)

        def evac_probs(eng, A, u, copy):
            full(eng, A.jt[u])
            if u >= 2:
                full(eng, A.jv[u - 2])
            w = A.width(u)
            free(copy(A.PT[:, u % 2, 0:w], banks[A.jt[u].bank][:, 0:w]), A.jt[u])

        def act_attention(act, A, extra=None):
            n = len(A.units)
            for t in range(n + 2):
                if t < n:
                    w = A.width(t)
                    if extra:
                        extra(t)
                    read(act, [A.js[t]])
                    act.activation(A.P[:, t % 3, 0:w], A.P[:, t % 3, 0:w], ACT.Exp, bias=negm[:, t:t + 1], scale=-1.0,
                                   accum_out=psums[:, t:t + 1]).then_inc(S("exp"), 1)
                    if A.sink:
                        act.activation(psink[:, t:t + 1], nsink[:, A.units[t][0]:A.units[t][0] + 1], ACT.Exp,
                                       bias=negm[:, t:t + 1], scale=-1.0).then_inc(S("sink_exp"), 1)
                if t >= 2 and (t - 2) % 2 == 0:
                    evac_probs(act, A, t - 2, lambda o, i: act.activation(o, i, ACT.Copy))

        def dve_attention(v, A, chain, before=None):
            n = len(A.units)
            for t in range(n + 3):
                if t < n:
                    w = A.width(t)
                    if before:
                        before(t)
                    full(v, A.js[t])
                    if t >= 3:
                        full(v, A.jt[t - 3])
                    init = nsink[:, A.units[t][0]:A.units[t][0] + 1] if A.sink else BIG
                    free(v.tensor_tensor_reduce(A.P[:, t % 3, 0:w], banks[A.js[t].bank][:, 0:w], A.added(t), 1.0, init,
                                                ALU.add, ALU.min, negm[:, t:t + 1]), A.js[t])
                if 0 <= t - 2 < n and (t - 2) % 2 == 1:
                    evac_probs(v, A, t - 2, lambda o, i: v.tensor_copy(o, i))
                if t >= 3:
                    u = t - 3
                    v.wait_ge(S("exp"), A.base + u + 1)
                    if A.sink:
                        v.wait_ge(S("sink_exp"), u + 1)
                        chain(v.tensor_tensor(psums[:, u:u + 1], psums[:, u:u + 1], psink[:, u:u + 1], ALU.add))
                    chain(v.reciprocal(precip[:, u:u + 1], psums[:, u:u + 1]))
                    full(v, A.jv[u])
                    free(v.tensor_scalar(A.outp(u), banks[A.jv[u].bank][:, 0:HD], precip[:, u:u + 1], None, ALU.mult),
                         A.jv[u])

        units = [(h, i) for h in range(H1) for i in range(NT)]
        head_rows = lambda h: slice(HD * (h % 2), HD * (h % 2) + HD)

        o_fox = o_tok
        FOX = Attention(
            "fox", units,
            q=lambda u: qfT[head_rows(units[u][0]), units[u][0] // 2, P * units[u][1]:P * (units[u][1] + 1)],
            k=lambda u: kfT[head_rows(units[u][0]), units[u][0] // 2, 0:P * (units[u][1] + 1)],
            v=lambda u, b: vf[:, b, HD * units[u][0]:HD * (units[u][0] + 1)],
            added=lambda u: decay_row[units[u][0] % 2][:, 0:P * (units[u][1] + 1)],
            width=lambda u: P * (units[u][1] + 1), keys=None,
            outp=lambda u: o_fox[:, units[u][1], HD * units[u][0]:HD * (units[u][0] + 1)], mask_by_pe=True)
        o_swa = vf
        SWA = Attention(
            "swa", units,
            q=lambda u: qsT[head_rows(units[u][0]), units[u][0] // 2, P * units[u][1]:P * (units[u][1] + 1)],
            k=lambda u: ksT[head_rows(units[u][0]), units[u][0] // GRP, P * max(units[u][1] - 1, 0):P * (units[u][1] + 1)],
            v=lambda u, b: vs[:, max(units[u][1] - 1, 0) + b, HD * (units[u][0] // GRP):HD * (units[u][0] // GRP + 1)],
            added=lambda u: C("window")[:, 0:2 * P] if units[u][1] else C("window")[:, P:2 * P],
            width=lambda u: 2 * P if units[u][1] else P, keys=None,
            outp=lambda u: o_swa[:, units[u][1], HD * units[u][0]:HD * (units[u][0] + 1)], sink=True)
        mqT, mkT = av(0, 4096, ML_H), av(4096, 4096, ML_H)
        mv = av(8192, 2048, NT)
        o_mla = o_tok
        MLA = Attention(
            "mla", units,
            q=lambda u: mqT[0:ML_QK, units[u][0], P * units[u][1]:P * (units[u][1] + 1)],
            k=lambda u: mkT[0:ML_QK, units[u][0], 0:P * (units[u][1] + 1)],
            v=lambda u, b: mv[:, b, ML_V * units[u][0]:ML_V * (units[u][0] + 1)],
            added=lambda u: C("causal")[:, T - P * (units[u][1] + 1):T],
            width=lambda u: P * (units[u][1] + 1), keys=None,
            outp=lambda u: o_mla[:, units[u][1], ML_V * units[u][0]:ML_V * (units[u][0] + 1)])
        MLA.P = av(10240, 1536, 3)
        MLA.PT = scratch[:, 2048:3072].rearrange("p (a b) -> p a b", a=2)

        TWO_PI = 2.0 * np.pi
        C1 = 6.28125
        C2 = float(np.float32(TWO_PI - C1).view(np.uint32) & np.uint32(0xFFFFF000))
        C2 = float(np.array([np.float32(TWO_PI - C1).view(np.uint32) & np.uint32(0xFFFFF000)], np.uint32).view(np.float32)[0])
        C3 = float(np.float32(TWO_PI - C1 - C2))
        ROUND = 12582912.0

        def dve_angles(v, chain, name, inv, cos_t, sin_t, pos, ang_t, k_t):
            chain(v.tensor_scalar(ang_t, pos, inv, None, ALU.mult))
            for dst, turn, shift in ((cos_t, 0.25, np.pi / 2), (sin_t, 0.0, 0.0)):
                chain(v.tensor_scalar(k_t, ang_t, 1.0 / TWO_PI, turn, ALU.mult, ALU.add))
                chain(v.tensor_scalar(k_t, k_t, ROUND, None, ALU.add))
                chain(v.tensor_scalar(k_t, k_t, ROUND, None, ALU.subtract))
                chain(v.scalar_tensor_tensor(dst, k_t, -C1, ang_t, ALU.mult, ALU.add))
                chain(v.scalar_tensor_tensor(dst, k_t, -C2, dst, ALU.mult, ALU.add))
                chain(v.scalar_tensor_tensor(dst, k_t, -C3, dst, ALU.mult, ALU.add))
                if shift:
                    chain(v.tensor_scalar(dst, dst, shift, None, ALU.add))
                chain(v.tensor_scalar(dst, dst, 3.1415925, -3.1415925, ALU.min, ALU.max))
            v.sem_inc(S("angles"), 1)

        def act_sines(act, name, cos_t, sin_t):
            act.wait_ge(S("angles"), ROPES[name])
            act.activation(cos_t, cos_t, ACT.Sin).then_inc(S("sines"), 1)
            act.activation(sin_t, sin_t, ACT.Sin).then_inc(S("sines"), 1)

        def dve_rope(v, chain, job, dst, cos_t, sin_t, t, rows=slice(0, P)):
            full(v, job)
            v.tensor_tensor(t[rows], banks[job.bank][rows, :], sin_t[rows], ALU.mult).then_inc(S("rope_t"), 1)
            S_count["rope"] += 1
            chain(v.tensor_tensor(dst, dst, cos_t[rows], ALU.mult))
            v.wait_ge(S("rope_t"), S_count["rope"])
            free(v.tensor_tensor(dst, dst, t[rows], ALU.add), job)

        S_count = {"rope": 0}

        m_filled = {k: sem("m_got_" + k) for k in ("xT", "h1", "h3", "aT", "y")}
        m_arr = [sem(f"m_arr{k}") for k in range(6)]
        m_hi = [sem(f"m_hi{m}") for m in range(3)]
        m_lo = [sem(f"m_lo{m}") for m in range(3)]
        m_xhi, m_x = sem("m_xhi"), sem("m_x")
        m_ahi, m_a = sem("m_ahi"), sem("m_a")
        m_silu, m_act, m_y = sem("m_silu"), sem("m_act"), sem("m_y")
        m_gather, m_scatter, m_idx = sem("m_gather"), sem("m_scatter"), sem("m_idx")
        m_done, m_ready, m_go, m_pe_go = sem("m_done"), sem("m_ready"), sem("m_go"), sem("m_pe_go")
        XTb, H1b, H3b, ATb, Y0b, Y1b = banks[0:6]
        tok_tab = scratch[0:BLK, 0:NE * EB].bitcast(I32)
        asg_tab = scratch[0:BLK, 1024:1024 + NE * EB].bitcast(I32)
        idx_t = scratch[0:BLK, 2048:2049].bitcast(I32)
        idx_a = scratch[0:BLK, 2049:2050].bitcast(I32)
        Xe = scratch[0:BLK, 2056:3080]
        y_b = side[0:BLK, 768:1792]
        silu_b = side[0:BLK, 1792:2304]
        act_b = side[0:BLK, 2304:2816]
        blk = small[0:1, 40:296].bitcast(I32)
        h2, h2T = av(4096, 4096, NT), av(8192, 4096, DC)
        row_gain = side[:, 0:1024]
        w_r = side[:, 1024:1024 + DC * NR].rearrange("p (c n) -> p c n", c=DC)
        r_row = side[:, 1600:1600 + NR]
        rcst = side[:, 1696:1696 + 128]
        logit = side[:, 2208:2208 + NT * NR].rearrange("p (i n) -> p i n", n=NR)
        onehot = side[:, 2496:2496 + 2 * NT * NE].rearrange("p (i k n) -> p i k n", i=NT, k=2)
        both = side[:, 3008:3008 + NT * NE].rearrange("p (i n) -> p i n", n=NE)
        rwork = scratch[:, 3080:4096]
        pos_t = av(2100, 8).bitcast(I32)
        id_t = av(2108, 8).bitcast(I32)
        sentinel = av(2200, 256).bitcast(I32)
        ids_raw = av(2460, 256, 8).bitcast(I32)
        ids_f = av(2720, 256, 8)

        rqT, rkT, rgT = av(0, 2048, 4), av(2048, 2048, 4), av(6144, 2048, 4)
        rv = av(4096, 2048, NT)
        lat = av(8192, 2560, NT)
        decays = scratch[:, 0:2048].rearrange("p (h c) -> p h c", h=RH)
        cos2, sin2 = scratch[:, 2048:2560], scratch[:, 2560:3072]
        tmp2 = scratch[:, 3072:3584]
        pos2 = scratch[:, 3584:4096]
        ang2 = av(10752, 512)
        krot = av(11264, 512)
        k2 = av(11776, 512)
        sT = [av(10752, 512), av(11776, 512)]
        o_flat = o_tok[:, :, :].rearrange("p a b -> p (a b)")
        cos3, sin3, ang3, k3 = [o_flat[:, 512 * k:512 * (k + 1)] for k in range(4)]
        cqT, ckvT = chunks_of(hTh, hTl), chunks_of(hTh, hTl, QL // P)
        catT = tuple(lambda c, f=f, g=g: f(c) if c < 4 else g(c - 4) for f, g in zip(ofT, osT))
        mixo = av(4096, 4096, NT)
        gtmp = [scratch[:, 512 * k:512 * (k + 1)] for k in range(2)]
        gain_mix = scratch[:, 1024:2048]
        gain_ffn, gain_ple, bias_ple = rows[:, 0, :], rows[:, 1, :], rows[:, 2, :]
        p_tok = rows[:, 3, :].rearrange("p (a b) -> p a b", a=NT)

        def ff_lo(f):
            return ffl0[:, f, :] if f < 8 else ffl1[:, f - 8, :]

        ffT = (lambda c: ffh[:, c, :]), ff_lo
        hT5, pT = (ffh[:, 0:8, :], ffh[:, 8:16, :]), (ffh[:, 16:18, :], ffh[:, 18:20, :])
        e_tok = scratch[:, :].rearrange("p (a b) -> p a b", a=NT)
        pg_out = side[:, :].rearrange("p (a b) -> p a b", a=NT)

        mix_scaled = at("mix_scaled", F0 + 8192, [NT, D])

        def mixg(i):
            return mix_scaled[:, i, :]

        def xn6(i):
            return av(8192 + 1024 * i, 1024)

        NX = 2 * NBLK

        def pe_second(pe, heads_to_feature):
            pe.wait_ge(S("xn4"), NT)
            pe_to_feature(pe, J["hT3"], lambda i, c: xn(i)[:, P * c:P * (c + 1)])
            read(pe, J["hT3"])
            pe_feature(pe, "rq", hT)
            pe_feature(pe, "rk", hT)
            for name, t in (("rq", rqT), ("rk", rkT)):
                read(pe, J[name])
                for c, job in enumerate(J[name + "_rot"]):
                    claim(pe, job)
                    fill(pe.matmul(banks[job.bank][:, :], C("rot_ret"), t[:, c, :], start=True, stop=True), job)
            pe_token(pe, "rv", hT)
            pe_feature(pe, "rg", hT)
            pe_token(pe, "lat0", hT)
            u = units_of["lat1"][0]
            loaded(pe, u)
            wh, wl = parts(u)
            for i, job in enumerate(J["lat1"]):
                claim(pe, job)
                t = slice(P * i, P * (i + 1))
                for c in range(DC):
                    mm = three(pe, banks[job.bank][:, 0:P], (hTh[:, c, t], hTl[:, c, t]),
                               (wh[:, c, 0:P], wl[:, c, 0:P]), c == 0, c == DC - 1)
                fill(mm, job)
            job = J["kr"][0]
            claim(pe, job)
            for c in range(DC):
                mm = three(pe, banks[job.bank][0:ML_QK, :], (wh[:, c, 64:64 + ML_QK], wl[:, c, 64:64 + ML_QK]),
                           (hTh[:, c, :], hTl[:, c, :]), c == 0, c == DC - 1)
            fill(mm, job)
            read(pe, J["rq_rot"] + J["rk_rot"] + J["rv"])
            for h in range(RH):
                for j in range(NT + 1):
                    if j < NT:
                        job = J["ret_s"][NT * h + j]
                        claim(pe, job)
                        fill(pe.matmul(banks[job.bank][:, 0:T - P * j], rkT[:, h, P * j:P * (j + 1)], rqT[:, h, P * j:T],
                                       start=True, stop=True), job)
                    if j >= 1:
                        job = J["ret_v"][h]
                        if j == 1:
                            claim(pe, job)
                        read(pe, [J["ret_s"][NT * h + j - 1]])
                        mm = pe.matmul(banks[job.bank][:, P * (j - 1):T], rv[:, j - 1, P * h:P * (h + 1)],
                                       sT[(j - 1) % 2][:, 0:T - P * (j - 1)], start=(j == 1), stop=(j == NT))
                        if j < NT:
                            mm.then_inc(S("ret_used"), 1)
                fill(mm, J["ret_v"][h])
            for h in range(RH):
                job = J["ret_m"][h]
                claim(pe, job)
                read(pe, [J["ret_v"][h]])
                fill(pe.matmul(banks[job.bank][:, :], C("ones"), rqT[:, h, :], start=True, stop=True), job)
            for h in range(RH):
                job = J["ret_m"][RH + h]
                claim(pe, job)
                pe.wait_ge(S("ret_sq"), h + 1)
                fill(pe.matmul(banks[job.bank][:, :], C("ones"), rkT[:, h, :], start=True, stop=True), job)
            pe.wait_ge(S("latn"), 2 * NT)
            pe_to_feature(pe, J["cqT"], lambda i, c: lat[:, i, P * c:P * (c + 1)])
            pe_to_feature(pe, J["ckvT"], lambda i, c: lat[:, i, QL + P * c:QL + P * (c + 1)])
            read(pe, J["kr"])
            job = J["kr_rot"][0]
            claim(pe, job)
            fill(pe.matmul(banks[job.bank][0:ML_QK, :], C("rot_mla")[0:ML_QK, 0:ML_QK], krot[0:ML_QK], start=True,
                           stop=True), job)
            read(pe, J["cqT"] + J["ckvT"])
            J["uq"] = J["mq"]
            pe_feature(pe, "uq", cqT, ML_QK, ML_QK)
            read(pe, J["mq"])
            for h, job in enumerate(J["mq_rot"]):
                claim(pe, job)
                fill(pe.matmul(banks[job.bank][0:ML_QK, :], C("rot_mla")[0:ML_QK, 0:ML_QK], mqT[0:ML_QK, h, :],
                               start=True, stop=True), job)
            u = units_of["ukv"][0]
            loaded(pe, u)
            wh, wl = parts(u)
            for h, job in enumerate(J["mk"]):
                claim(pe, job)
                k = slice(P * h, P * (h + 1))
                for c in range(2):
                    mm = three(pe, banks[job.bank][:, :], (wh[:, c, k], wl[:, c, k]), (ckvT[0](c), ckvT[1](c)),
                               c == 0, c == 1)
                fill(mm, job)
            values = [w.rearrange("p c (h n) -> p c h n", h=ML_H)[:, :, :, ML_N:ML_N + ML_V] for w in (wh, wl)]
            for i, job in enumerate(J["mv"]):
                claim(pe, job)
                t = slice(P * i, P * (i + 1))
                for c in range(2):
                    mm = three(pe, banks[job.bank][:, :].rearrange("p (h n) -> p h n", h=ML_H),
                               (ckvT[0](c)[:, t], ckvT[1](c)[:, t]), (values[0][:, c], values[1][:, c]), c == 0, c == 1)
                fill(mm, job)
            read(pe, J["mq_rot"] + J["mk"] + J["mv"])
            pe.wait_ge(S("krows"), ML_H)
            pe_attention(pe, MLA)
            heads_to_feature("mla_oT", MLA, o_mla)
            read(pe, J["mla_oT"])
            pe.wait_ge(S("ret_out"), RH)
            for n in range(2):
                pe_token(pe, f"o{n}", catT)
            pe.wait_ge(S("xn6"), NT)
            pe_to_feature(pe, J["hT4"], lambda i, c: xn6(i)[:, P * c:P * (c + 1)])
            read(pe, J["hT4"])
            for n in range(n_ff):
                for k in range(2):
                    for name in ("gate", "up"):
                        u, job = units_of[name][n], J[name][2 * n + k]
                        if k == 0:
                            loaded(pe, u)
                        wh, wl = parts(u)
                        claim(pe, job)
                        for c in range(DC):
                            mm = three(pe, banks[job.bank][:, :], (wh[:, c, P * k:P * (k + 1)], wl[:, c, P * k:P * (k + 1)]),
                                       (hT[0](c), hT[1](c)), c == 0, c == DC - 1)
                        fill(mm, job)
            pe_token(pe, "down", ffT, lambda j: (j // 2, 512 * (j % 2)), lambda k: pe.wait_ge(S("ff"), 2 * (k + 1)))
            pe.wait_ge(S("w_p"), 16)
            pe_to_feature(pe, J["pT"], lambda i, c: p_tok[:, i, P * c:P * (c + 1)])
            read(pe, J["pT"])
            pe_token(pe, "ple", chunks_of(*pT), lambda j: (j % NT, 512 * (j // NT)))
            pe.wait_ge(S("x4"), NT)
            pe_to_feature(pe, J["hT5"], lambda i, c: x[:, i, P * c:P * (c + 1)])
            read(pe, J["hT5"])
            for n in range(2):
                pe_token(pe, f"pg{n}", chunks_of(*hT5))

        def dve_route(v, chain, before_tables):
            iota64, iota8 = rcst[:, 0:NE], rcst[:, NE:NE + NG]
            top = rwork[:, 48:56]
            topi = rwork[:, 56:64].bitcast(U32)
            gidx = rwork[:, 64:65]
            gsel = rwork[:, 72:80]
            masked = rwork[:, 128:192]
            place = rwork[:, 192:200]
            junk = rwork[:, 256:320]
            eidx = rwork[:, 80:88]
            for i, job in enumerate(J["router"]):
                full(v, job)
                free(v.tensor_tensor(logit[:, i, :], banks[job.bank][:, 0:NR], r_row, ALU.add), job)
                read(v, [job])
                g, e = logit[:, i, 0:NG], logit[:, i, NG:NR]
                chain(v.max(top, g))
                chain(v.max_index(topi, top, g))
                chain(v.tensor_copy(gidx, topi[:, 0:1]))
                v.tensor_scalar(rwork[:, 8 * i:8 * i + 8], g, top[:, 0:1], None, ALU.subtract).then_inc(S("r_g"), 1)
                v.wait_ge(S("r_g"), i + 1)
                chain(v.tensor_scalar(gsel, iota8, gidx, None, ALU.is_equal))
                chain(v.tensor_scalar(gsel, gsel, 1.0, BIG, ALU.subtract, ALU.mult))
                chain(v.tensor_tensor(masked.rearrange("p (g e) -> p g e", g=NG), e.rearrange("p (g e) -> p g e", g=NG),
                                      gsel.rearrange("p (g o) -> p g o", o=1).broadcast_to([P, NG, EG]), ALU.add))
                chain(v.max(top, masked))
                chain(v.max_index(topi, top, masked))
                chain(v.tensor_copy(eidx, topi))
                v.tensor_tensor(rwork[:, 40 + i:41 + i], top[:, 1:2], top[:, 0:1], ALU.subtract).then_inc(S("r_e"), 1)
                for k in range(2):
                    chain(v.tensor_scalar(onehot[:, i, k, :], iota64, eidx[:, k:k + 1], None, ALU.is_equal))
                v.wait_ge(S("r_e"), i + 1)
                v.tensor_tensor(both[:, i, :], onehot[:, i, 0, :], onehot[:, i, 1, :], ALU.add).then_inc(S("r_both"), 1)
                v.wait_ge(S("r_exp2"), i + 1)
                chain(v.scalar_tensor_tensor(rwork[:, 88:89], rwork[:, 40 + i:41 + i], 1.0, rwork[:, 32 + i:33 + i],
                                             ALU.add, ALU.mult))
                chain(v.reciprocal(gates[:, i, 0:1], rwork[:, 88:89]))
                chain(v.tensor_tensor(gates[:, i, 1:2], gates[:, i, 0:1], rwork[:, 40 + i:41 + i], ALU.mult))
                full(v, J["rank"][i])
                for k in range(2):
                    ins = v.tensor_tensor_reduce(junk, banks[J["rank"][i].bank][:, 0:NE], onehot[:, i, k, :], 1.0, 0.0,
                                                 ALU.mult, ALU.add, place[:, 2 + k:3 + k])
                    if k:
                        free(ins, J["rank"][i])
                    else:
                        chain(ins)
                read(v, [J["rank"][i]])
                for k in range(2):
                    chain(v.scalar_tensor_tensor(place[:, k:k + 1], eidx[:, k:k + 1], float(T), place[:, 2 + k:3 + k],
                                                 ALU.mult, ALU.add))
                for k in range(2):
                    v.tensor_copy(pos_t[:, NT * k + i:NT * k + i + 1], place[:, k:k + 1]).then_inc(S("r_pos"), 1)
            chain(v.tensor_copy(id_t[:, :], C("id2")))
            v.sem_inc(S("r_id"), 1)
            E = slice(0, NE)
            count, over, start = rwork[E, 256:257], rwork[E, 257:258], rwork[E, 258:260]
            full(v, J["count"][0])
            free(v.tensor_copy(count, banks[J["count"][0].bank][E, 0:1]), J["count"][0])
            read(v, J["count"])
            more = rwork[E, 272:272 + EB - 1]
            chain(v.tensor_scalar(more, rcst[E, 72:72 + EB - 1], count, None, ALU.is_lt))
            chain(v.tensor_reduce(over, more, AX.X, ALU.add))
            v.sem_inc(S("r_over"), 1)
            full(v, J["starts"][0])
            free(v.tensor_copy(start, banks[J["starts"][0].bank][E, 0:2]), J["starts"][0])
            read(v, J["starts"])
            rel, inside, low = [rwork[E, 320 + SPILL * k:320 + SPILL * (k + 1)] for k in range(3)]
            chain(v.tensor_scalar(rel, iota64[E, 0:SPILL], start[:, 0:1], None, ALU.subtract))
            chain(v.tensor_scalar(inside, rel, -0.5, None, ALU.is_gt))
            chain(v.tensor_scalar(low, rel, over, None, ALU.is_lt))
            chain(v.tensor_tensor(inside, inside, low, ALU.mult))
            chain(v.tensor_scalar(rel, rel, rcst[E, 96:97], None, ALU.add))
            v.tensor_tensor(low, inside, rel, ALU.mult).then_inc(S("r_further"), 1)
            bc = rwork[0:1, 512:512 + NBLK]
            chain(v.tensor_scalar(bc[:, 0:NE], iota64[0:1], float(EB), None, ALU.mult))
            full(v, J["further"][0])
            free(v.tensor_copy(bc[:, NE:NBLK], banks[J["further"][0].bank][0:1, 0:SPILL]), J["further"][0])
            read(v, J["further"])
            chain(v.tensor_copy(blk[0:1, 0:NBLK], bc))
            chain(v.tensor_scalar(blk[0:1, NBLK:NX], blk[0:1, 0:NBLK], 4, None, ALU.arith_shift_right))
            chain(v.tensor_scalar(gidx[0:1], start[0:1, 1:2], float(NE - 2), None, ALU.add))
            chain(v.tensor_copy(blk[0:1, NX:NX + 1], gidx[0:1]))
            before_tables()
            v.wait_ge(S("ids_in"), 16)
            chain(v.tensor_copy(ids_f, ids_raw))
            v.sem_inc(S("ids_f"), 1)
            for k, job in enumerate(J["ids"]):
                full(v, job)
                free(v.tensor_copy(asg_tab[:, 512 * k:512 * (k + 1)], banks[job.bank][0:BLK, :]), job)
            read(v, J["ids"])
            chain(v.tensor_scalar(tok_tab[:, :], asg_tab[:, :], 1, None, ALU.arith_shift_right))
            v.sem_inc(m_ready, 1)

        def dve_second(v, chain, evac):
            v.wait_ge(S("w_pos2"), 16)
            chain(v.tensor_copy(k2, pos2.bitcast(I32)))
            chain(v.tensor_copy(pos2, k2))
            dve_angles(v, chain, "rope2", C("inv_ret"), cos2, sin2, pos2, ang2, k2)
            dve_angles(v, chain, "rope3", C("inv_mla"), cos3, sin3, pos2, ang3, k3)
            for name in ("rq", "rk"):
                ahead(lo_until, v, name, len(J[name]) - 1)
            lo_until(v, units_of["rv"][1].n)
            v.wait_ge(S("sines"), 4)
            for name, t in (("rq", rqT), ("rk", rkT)):
                read(v, J[name])
                for c, job in enumerate(J[name + "_rot"]):
                    dve_rope(v, chain, job, t[:, c, :], cos2, sin2, tmp2)
                    read(v, [job])
            for name in ("rv", "rg", "lat0"):
                ahead(lo_until, v, name, len(J[name]) - 1)
            lo_until(v, units_of["uq"][0].n)
            job = J["kr"][0]
            full(v, job)
            free(v.tensor_copy(krot[0:ML_QK], banks[job.bank][0:ML_QK, :]), job)
            for h in range(RH):
                for j in range(NT):
                    job = J["ret_s"][NT * h + j]
                    full(v, job)
                    n = NT * h + j
                    if n >= 2:
                        m = n - 2
                        if m % NT == NT - 1:
                            full(v, J["ret_v"][m // NT])
                        else:
                            v.wait_ge(S("ret_used"), (m // NT) * (NT - 1) + m % NT + 1)
                    free(v.tensor_tensor(sT[j % 2][:, 0:T - P * j], banks[job.bank][:, 0:T - P * j],
                                         decays[:, h, 0:T - P * j], ALU.mult), job)
            dve_rstd(v, chain, "nq", ssq, rstd, NT, QL)
            dve_rstd(v, chain, "nk", ssq2, rstd2, NT, KVL)
            for i in range(NT):
                v.tensor_scalar(lat[:, i, 0:QL], lat[:, i, 0:QL], rstd[:, i:i + 1], None, ALU.mult).then_inc(S("latn"), 1)
                v.tensor_scalar(lat[:, i, QL:640], lat[:, i, QL:640], rstd2[:, i:i + 1], None,
                                ALU.mult).then_inc(S("latn"), 1)
            for h in range(RH):
                job = J["ret_m"][h]
                full(v, job)
                free(v.scalar_tensor_tensor(rqT[:, h, :], banks[job.bank][:, :], -1.0 / RD, rqT[:, h, :], ALU.mult,
                                            ALU.add), job)
                read(v, [job])
                v.sem_inc(S("ret_c"), 1)
            for h in range(RH):
                job = J["ret_m"][RH + h]
                full(v, job)
                free(v.tensor_scalar(rkT[:, h, :], banks[job.bank][:, :], 1.0 / RD, EPS, ALU.mult, ALU.add), job)
                read(v, [job])
                v.sem_inc(S("ret_var"), 1)
            dve_split_jobs(v, "cqT", hTh, hTl, lambda c: PRM("mla_q", c))
            dve_split_jobs(v, "ckvT", hTh, hTl, lambda c: PRM("mla_kv", c), QL // P)
            lo_until(v, units_of["uq"][1].n)
            for h in range(RH):
                v.wait_ge(S("ret_sd"), h + 1)
                chain(v.reciprocal(rkT[:, h, :], rkT[:, h, :]))
                chain(v.tensor_tensor(rqT[:, h, :], rqT[:, h, :], rkT[:, h, :], ALU.mult))
                chain(v.scalar_tensor_tensor(rqT[:, h, :], rqT[:, h, :], PRM("ret_gn", h), rgT[:, h, :], ALU.mult,
                                             ALU.mult))
                v.sem_inc(S("ret_f"), 1)
            for h in range(RH):
                dve_split(v, ("ret", h), ofTl[:, h, :], rqT[:, h, :], ofTh[:, h, :]).then_inc(S("ret_out"), 1)
            v.wait_ge(S("ret_out"), RH)
            v.wait_ge(S("sines"), 6)
            read(v, J["kr"])
            dve_rope(v, chain, J["kr_rot"][0], krot[0:ML_QK], cos3, sin3, tmp2, slice(0, ML_QK))
            read(v, J["kr_rot"])
            for h in range(ML_H):
                v.tensor_copy(mkT[ML_N:ML_QK, h, :], krot[ML_N:ML_QK]).then_inc(S("krows"), 1)
            read(v, J["mq"])
            lo_until(v, units_of["ukv"][0].n)
            for h, job in enumerate(J["mq_rot"]):
                dve_rope(v, chain, job, mqT[0:ML_QK, h, :], cos3, sin3, tmp2, slice(0, ML_QK))
                read(v, [job])
            read(v, J["mv"])
            lo_until(v, units_of["o0"][0].n)
            dve_attention(v, MLA, chain)
            lo_until(v, units_of["o0"][1].n)
            dve_split_jobs(v, "mla_oT", osTh, osTl)
            for name in ("o0", "o1"):
                ahead(lo_until, v, name)
            v.wait_ge(S("w_gm"), 16)
            for n in range(2):
                for i, job in enumerate(J[f"o{n}"]):
                    cols = slice(512 * n, 512 * (n + 1))
                    read(v, [job])
                    v.tensor_tensor(mixg(i)[:, cols], mixo[:, i, cols], gain_mix[:, cols], ALU.mult).then_inc(S("mixg"), 1)
            dve_rstd(v, chain, "n5", ssq, rstd, NT, D)
            v.wait_ge(S("mixg"), 2 * NT)
            for i in range(NT):
                v.scalar_tensor_tensor(x[:, i, :], mixg(i), rstd[:, i:i + 1], x[:, i, :], ALU.mult,
                                       ALU.add).then_inc(S("x3"), 1)
            dve_rstd(v, chain, "n6", ssq2, rstd2, NT, D)
            v.wait_ge(S("x3"), NT)
            for i in range(NT):
                v.tensor_scalar(xn6(i), x[:, i, :], rstd2[:, i:i + 1], None, ALU.mult).then_inc(S("xn6"), 1)
            dve_split_jobs(v, "hT4", hTh, hTl, lambda c: PRM("pre_ffn", c))
            lo_until(v, units_of["up"][0].n)
            for f, job in enumerate(J["up"]):
                if f % 2 == 1 and f + 1 < FC:
                    lo_until(v, units_of["gate"][f // 2 + 1].n)
                full(v, job)
                read(v, [J["gate"][f]])
                g = gtmp[f % 2]
                free(v.tensor_tensor(g, g, banks[job.bank][:, :], ALU.mult), job)
                read(v, [job])
                if f == 0:
                    v.wait_ge(S("xn6"), NT)
                dve_split(v, ("ff", f), ff_lo(f), g, ffh[:, f, :]).then_inc(S("ff"), 1)
                if f % 2 == 1 and f + 1 < FC:
                    lo_until(v, units_of["up"][f // 2 + 1].n)
            ahead(lo_until, v, "down")
            for k in range(1, 8, 2):
                job = J["down"][k]
                full(v, job)
                free(v.tensor_copy(ffo[:, k // 2, 512:1024], banks[job.bank][:, :]), job)
            dve_split_jobs(v, "pT", *pT)
            ahead(lo_until, v, "ple")
            dve_rstd(v, chain, "n7", ssq, rstd, NT, D)
            v.wait_ge(S("w_gf"), 16)
            for i in range(NT):
                chain(v.scalar_tensor_tensor(ffo[:, i, :], ffo[:, i, :], rstd[:, i:i + 1], gain_ffn, ALU.mult, ALU.mult))
                v.tensor_tensor(x[:, i, :], x[:, i, :], ffo[:, i, :], ALU.add).then_inc(S("x4"), 1)
            dve_rstd(v, chain, "n8", ssq2, rstd2, NT, D)
            v.wait_ge(S("w_gp"), 16)
            for i in range(NT):
                v.scalar_tensor_tensor(e_tok[:, i, :], e_tok[:, i, :], rstd2[:, i:i + 1], gain_ple, ALU.mult,
                                       ALU.mult).then_inc(S("e_tok"), 1)
            dve_split_jobs(v, "hT5", *hT5)
            ahead(lo_until, v, "pg0")
            v.wait_ge(S("w_bp"), 16)
            for k in range(2 * NT):
                n, i = k // NT, k % NT
                job = J[f"pg{n}"][i]
                ahead(lo_until, v, f"pg{n}")
                full(v, job)
                cols = slice(512 * n, 512 * (n + 1))
                v.tensor_tensor(pg_out[:, i, cols], banks[job.bank][:, :], bias_ple[:, cols], ALU.add).then_inc(S("pg"), 1)
            v.wait_ge(S("e_tok"), NT)
            v.wait_ge(S("x4"), NT)
            for i in range(NT):
                for n in range(2):
                    k = NT * n + i
                    cols = slice(512 * n, 512 * (n + 1))
                    v.wait_ge(S("pg_s"), NT + i + 1 if n else i + 1)
                    chain(v.tensor_tensor(pg_out[:, i, cols], pg_out[:, i, cols], e_tok[:, i, cols], ALU.mult))
                    v.tensor_tensor(x[:, i, cols], x[:, i, cols], pg_out[:, i, cols], ALU.add).then_inc(S("final"), 1)

        def ring_y(i):
            return arena[:, 2048 * i:2048 * (i + 1)].rearrange("p (k n) -> p k n", k=2)

        def act_second(act, chain, row):
            act_sines(act, "rope2", cos2, sin2)
            act_sines(act, "rope3", cos3, sin3)
            for c, job in enumerate(J["rq"]):
                ahead(hi_until, act, "rq", c)
                full(act, job)
                if c == 0:
                    act.wait_ge(S("n3x"), NT)
                free(act.activation(rqT[:, c, :], banks[job.bank][:, :], ACT.Copy), job)
            for c, job in enumerate(J["rk"]):
                ahead(hi_until, act, "rk", c)
                full(act, job)
                free(act.activation(rkT[:, c, :], banks[job.bank][:, :], ACT.Copy, scale=RD ** -0.5), job)
            for i, job in enumerate(J["rv"]):
                ahead(hi_until, act, "rv", i)
                full(act, job)
                free(act.activation(rv[:, i, :], banks[job.bank][:, :], ACT.Copy), job)
            for c, job in enumerate(J["rg"]):
                ahead(hi_until, act, "rg", c)
                full(act, job)
                free(act.activation(rgT[:, c, :], banks[job.bank][:, :], ACT.Silu), job)
            for i, job in enumerate(J["lat0"]):
                ahead(hi_until, act, "lat0", i)
                full(act, job)
                free(act.activation(lat[:, i, 0:512], banks[job.bank][:, :], ACT.Copy), job)
            for i, job in enumerate(J["lat1"]):
                full(act, job)
                free(act.activation(lat[:, i, 512:640], banks[job.bank][:, 0:128], ACT.Copy), job)
            hi_until(act, units_of["uq"][0].n)
            read(act, J["lat0"] + J["lat1"])
            act_sumsq(act, chain, "nq", lambda i: lat[:, i, 0:QL], NT, tmp2[:, 0:QL], ssq)
            act_sumsq(act, chain, "nk", lambda i: lat[:, i, QL:QL + KVL], NT, tmp2[:, 0:KVL], ssq2)
            for h in range(RH):
                full(act, J["ret_v"][h])
                free(act.activation(rqT[:, h, :], banks[J["ret_v"][h].bank][:, :], ACT.Copy), J["ret_v"][h])
            act_sqrt(act, "nq", rstd, NT)
            act_sqrt(act, "nk", rstd2, NT)
            for h in range(RH):
                act.wait_ge(S("ret_c"), h + 1)
                act.activation(rkT[:, h, :], rqT[:, h, :], ACT.Square).then_inc(S("ret_sq"), 1)
            for h in range(RH):
                act.wait_ge(S("ret_var"), h + 1)
                act.activation(rkT[:, h, :], rkT[:, h, :], ACT.Sqrt).then_inc(S("ret_sd"), 1)
            hi_until(act, units_of["uq"][1].n)
            act_split_jobs(act, "cqT", hTh, lambda c: PRM("mla_q", c))
            act_split_jobs(act, "ckvT", hTh, lambda c: PRM("mla_kv", c), QL // P)
            for h in range(RH):
                act.wait_ge(S("ret_f"), h + 1)
                act_split(act, ("ret", h), ofTh[:, h, :], rqT[:, h, :])
            for h, job in enumerate(J["mq"]):
                full(act, job)
                if h == 0:
                    act.wait_ge(S("ret_out"), RH)
                free(act.activation(mqT[0:ML_QK, h, :], banks[job.bank][0:ML_QK, :], ACT.Copy, scale=-(ML_QK ** -0.5)), job)
            hi_until(act, units_of["ukv"][0].n)
            for h, job in enumerate(J["mk"]):
                full(act, job)
                free(act.activation(mkT[0:ML_N, h, :], banks[job.bank][0:ML_N, :], ACT.Copy), job)
            for i, job in enumerate(J["mv"]):
                full(act, job)
                free(act.activation(mv[:, i, :], banks[job.bank][:, :], ACT.Copy), job)
            hi_until(act, units_of["o0"][0].n)
            act_attention(act, MLA)
            hi_until(act, units_of["o0"][1].n)
            act_split_jobs(act, "mla_oT", osTh)
            read(act, J["mla_oT"])
            row(gain_mix, "post_mix_norm_2", D, S("w_gm"))
            for n in range(2):
                ahead(hi_until, act, f"o{n}")
                for i, job in enumerate(J[f"o{n}"]):
                    full(act, job)
                    if n == 0 and i == 0:
                        read(act, J["mla_oT"])
                    free(act.activation(mixo[:, i, 512 * n:512 * (n + 1)], banks[job.bank][:, :], ACT.Copy), job)
                    if n == 1:
                        read(act, [J["o0"][i], job])
                        ins = act.activation(arena[:, 8192:8192 + D], mixo[:, i, :], ACT.Square,
                                             accum_out=ssq[:, i:i + 1])
                        chain(ins)
            act.sem_inc(S("norm_squares"), 1)
            act_sqrt(act, "n5", rstd, NT)
            act_sumsq(act, chain, "n6", lambda i: x[:, i, :], NT, arena[:, 8192:8192 + D], ssq2,
                      lambda i: act.wait_ge(S("x3"), i + 1))
            act_sqrt(act, "n6", rstd2, NT)
            act_split_jobs(act, "hT4", hTh, lambda c: PRM("pre_ffn", c))
            hi_until(act, units_of["up"][0].n)
            for f, job in enumerate(J["gate"]):
                full(act, job)
                if f >= 2:
                    act.wait_ge(S("ff"), f - 1)
                free(act.activation(gtmp[f % 2], banks[job.bank][:, :], ACT.Silu), job)
                if f % 2 == 1 and f + 1 < FC:
                    hi_until(act, units_of["gate"][f // 2 + 1].n)
                read(act, [J["up"][f]])
                act_split(act, ("ff", f), ffh[:, f, :], gtmp[f % 2])
                if f % 2 == 1 and f + 1 < FC:
                    hi_until(act, units_of["up"][f // 2 + 1].n)
            full(act, J["up"][-1])
            row(gain_ffn, "post_ffn_norm_2", D, S("w_gf"))
            row(gain_ple, "ple_norm_2", D, S("w_gp"))
            row(bias_ple, "b_ple_gate_2", D, S("w_bp"))
            act.dma_start(p_tok, a["p_2"][0, 0].rearrange("(i p) n -> p i n", p=P)).then_inc(S("w_p"), 16)
            ahead(hi_until, act, "down")
            for k in range(0, 8, 2):
                job = J["down"][k]
                full(act, job)
                free(act.activation(ffo[:, k // 2, 0:512], banks[job.bank][:, :], ACT.Copy), job)
            act_split_jobs(act, "pT", pT[0])
            ahead(hi_until, act, "ple")
            read(act, J["down"])
            act_sumsq(act, chain, "n7", lambda i: ffo[:, i, :], NT, arena[:, 10240:10240 + D], ssq)
            act_sqrt(act, "n7", rstd, NT)
            for k, job in enumerate(J["ple"]):
                full(act, job)
                free(act.activation(e_tok[:, k % NT, 512 * (k // NT):512 * (k // NT) + 512], banks[job.bank][:, :],
                                    ACT.Copy), job)
            read(act, J["ple"])
            act_sumsq(act, chain, "n8", lambda i: e_tok[:, i, :], NT, arena[:, 10240:10240 + D], ssq2)
            act_sqrt(act, "n8", rstd2, NT)
            act_split_jobs(act, "hT5", hT5[0])
            ahead(hi_until, act, "pg0")
            ahead(hi_until, act, "pg1")
            for k in range(2 * NT):
                act.wait_ge(S("pg"), k + 1)
                v = pg_out[:, k % NT, 512 * (k // NT):512 * (k // NT) + 512]
                act.activation(v, v, ACT.Sigmoid).then_inc(S("pg_s"), 1)

        @block.sync
        def _(sp):
            def load(n):
                if n >= RAW:
                    sp.wait_ge(lo_made, n - RAW + 1)
                u = order[n]
                dst = raw[:, n % RAW, 0:u.chunks * u.cols].rearrange("p (c n) -> p c n", c=u.chunks)
                k = u.cols // u.copies
                for j in range(u.copies):
                    sp.dma_start(dst[:, :, k * j:k * (j + 1)], u.src).then_inc(arrived[n % RAW], 16)

            for i in range(NT):
                sp.dma_start(x[:, i, :], a["x"][0, P * i:P * (i + 1), :]).then_inc(s_x[i], 16)
            for n in range(n_first):
                load(n)
            if stop <= 1:
                return
            full(sp, order[n_first - 1].last)
            weights = (a["w1"][0], a["w3"][0], a["w2"][0])

            def load_half(m, h, expert):
                k = 2 * m + h
                nc_ = 8 if m < 2 else 4
                w = weights[m][expert, :, :] if isinstance(expert, int) else weights[m][bass.ds(expert, 1), :, :]
                pat = "(p c) n -> p c n" if isinstance(expert, int) else "a (p c) n -> p (a c) n"
                src = w.rearrange(pat, p=P)[:, h * nc_ // 2:(h + 1) * nc_ // 2, :]
                dst = m_raw[:, k, :].rearrange("p (c n) -> p c n", c=nc_ // 2)
                sp.dma_start(dst, src).then_inc(m_arr[k], 16)

            for m in (0, 1):
                for h in range(2):
                    load_half(m, h, 0)
            for h in range(2):
                sp.wait_ge(m_lo[0], h + 1)
                load_half(0, h, 1)
            sp.wait_ge(m_ready, 1)
            count = sp.value_load(blk[0:1, NX:NX + 1], min_val=NE - 2, max_val=NBLK - 2)
            EX = NBLK

            def load_block(i, last):
                e0 = sp.value_load(blk[0:1, bass.ds(i + EX, 1)], min_val=0, max_val=NE - 1)
                e1 = sp.value_load(blk[0:1, bass.ds(i + (EX + 1), 1)], min_val=0, max_val=NE - 1)
                if not last:
                    e2 = sp.value_load(blk[0:1, bass.ds(i + (EX + 2), 1)], min_val=0, max_val=NE - 1)
                for h in range(2):
                    sp.wait_ge(m_lo[1], 2 * i + (h + 1))
                    load_half(1, h, e1)
                for h in range(2):
                    sp.wait_ge(m_lo[2], 2 * i + (h + 1))
                    load_half(2, h, e0)
                if not last:
                    for h in range(2):
                        sp.wait_ge(m_lo[0], 2 * i + (h + 3))
                        load_half(0, h, e2)

            with sp.Fori(0, count) as i:
                load_block(i, False)
            load_block(count, True)
            e0 = sp.value_load(blk[0:1, bass.ds(count + (EX + 1), 1)], min_val=0, max_val=NE - 1)
            for h in range(2):
                sp.wait_ge(m_lo[2], 2 * count + (h + 3))
                load_half(2, h, e0)
            if stop <= 2:
                return
            for n in range(n_first, n_first + RAW):
                if n == n_first:
                    sp.wait_ge(m_lo[0], 2 * count + 4)
                    sp.wait_ge(m_lo[1], 2 * count + 4)
                load(n)
            for n in range(n_first + RAW, len(order)):
                load(n)
            o = out[0].rearrange("(i p) n -> p i n", p=P)
            for i in range(NT):
                sp.wait_ge(S("final"), 2 * (i + 1))
                sp.dma_start(o[:, i, :], x[:, i, :]).then_inc(S("stored"), 16)
            sp.wait_ge(S("stored"), 16 * NT)

        @block.scalar
        def _(act):
            chain = Chain(act, act_own)

            def row(dst, name, n, s, off=0):
                t = a[name]
                act.dma_start(dst, bass.AP(tensor=t.tensor, offset=off, ap=[[0, P], [1, n]])).then_inc(s, 16)

            act.dma_start(cst[:, :], a["consts"]).then_inc(s_const, 16)
            act.dma_start(prm[:, :], a["params"]).then_inc(s_const, 16)
            row(bf_row, "b_forget", H1, s_const)
            row(sink_row, "attn_sinks", H1, s_const)
            act.dma_start(w_f, cols_of(win, CF, CF + H1)).then_inc(s_wf, 16)
            row(pos_i, "positions", T, s_pos)

            act_sumsq(act, chain, "n1", lambda i: x[:, i, :], NT, arena[:, 0:D], ssq,
                      lambda i: act.wait_ge(s_x[i], 16))
            act_sqrt(act, "n1", rstd, NT)
            hi_until(act, 1)
            act_split_jobs(act, "hT1", hTh, lambda c: PRM("attn_norm", c))
            act.wait_ge(s_wf, 16)
            act_split(act, "w_f", wf_h[:, :, :], w_f)
            full(act, J["zT"][0])
            free(act.activation(zT, banks[J["zT"][0].bank][0:H1, :], ACT.Copy), J["zT"][0])
            for c, job in enumerate(J["qs"]):
                ahead(hi_until, act, "qs", c)
                full(act, job)
                free(act.activation(qsT[:, c, :], banks[job.bank][:, :], ACT.Copy, scale=-(HD ** -0.5)), job)
            ahead(hi_until, act, "ks", 0)
            act.wait_ge(S("f_abs"), 1)
            act.activation(logf_t, logf_t, ACT.Exp, scale=-1.0).then_inc(S("f_exp"), 1)
            act.wait_ge(S("f_one"), 1)
            act.activation(logf_t, logf_t, ACT.Ln).then_inc(S("f_ln"), 1)
            ahead(hi_until, act, "ks", KVH - 1)
            act_sines(act, "rope1", cos1, sin1)
            for c, job in enumerate(J["qf"]):
                ahead(hi_until, act, "qf", c)
                full(act, job)
                free(act.activation(qfT[:, c, :], banks[job.bank][:, :], ACT.Copy, scale=-(HD ** -0.5)), job)
            hi_until(act, units_of["vs"][0].n)
            full(act, J["cT"][0])
            act.wait_ge(S("posdone"), 1)
            free(act.activation(cT, banks[J["cT"][0].bank][0:H1, :], ACT.Copy), J["cT"][0])
            hi_until(act, units_of["vf"][0].n)
            for i, job in enumerate(J["vs"]):
                full(act, job)
                free(act.activation(vs[:, i, :], banks[job.bank][:, 0:KVH * HD], ACT.Copy), job)
            ahead(hi_until, act, "vf")
            for i, job in enumerate(J["vf"]):
                full(act, job)
                free(act.activation(vf[:, i, :], banks[job.bank][:, :], ACT.Copy), job)

            def decay(t):
                if t % NT == 0:
                    h = t // NT
                    if h == 0:
                        act.wait_ge(S("posdone"), 1)
                    if h >= 2:
                        read(act, [FOX.js[NT * (h - 1) - 1]])
                    full(act, J["decay"][h])
                    free(act.activation(decay_row[h % 2], banks[J["decay"][h].bank][:, :], ACT.Copy), J["decay"][h])

            hi_until(act, units_of["gf"][1].n)
            act_attention(act, FOX, decay)

            act_attention(act, SWA)
            act_split_jobs(act, "swa_oT", osTh)
            act_split_jobs(act, "fox_oT", ofTh)
            for g, (name, dst) in enumerate((("gf", gfT), ("gs", gsT))):
                for c, job in enumerate(J[name]):
                    ahead(hi_until, act, name, c)
                    full(act, job)
                    if g == 0 and c == 0:
                        read(act, J["swa_oT"])
                    free(act.activation(dst[:, c, :], banks[job.bank][:, :], ACT.Sigmoid,
                                        bias=PRM("b_gate", 8 * g + c)), job)
            for name in ("pf", "ps"):
                ahead(hi_until, act, name, DC - 1)
            for c in range(DC):
                act.wait_ge(S("merged"), c + 1)
                act_split(act, ("merged", c), hTh[:, c, :], gfT[:, c, :])
            for n in range(2):
                ahead(hi_until, act, f"out{n}")
            full(act, J["ps"][-1])
            act.dma_start(w_r[:, :, 0:NG], cols_of(a["w_group"][0], 0, NG)).then_inc(S("w_r"), 16)
            act.dma_start(w_r[:, :, NG:NR], cols_of(a["w_expert"][0], 0, NE)).then_inc(S("w_r"), 16)
            row(row_gain, "ffn_norm", D, S("w_r"))
            row(r_row[:, 0:NG], "b_group", NG, S("w_r"))
            row(r_row[:, NG:NR], "b_expert", NE, S("w_r"))
            act.dma_start(rcst, a["route_consts"]).then_inc(S("w_r"), 16)
            act_sumsq(act, chain, "n2", lambda i: x[:, i, :], NT, arena[:, 8192:8192 + D], ssq,
                      lambda i: read(act, [J["out0"][i], J["out1"][i]]))
            act_sqrt(act, "n2", rstd, NT)
            for c, job in enumerate(J["hT2"]):
                if c % 2 == 0:
                    full(act, job)
                    free(act.activation(h2T[:, c, :], banks[job.bank][:, :], ACT.Copy), job)
            for i in range(NT):
                act.wait_ge(S("r_g"), i + 1)
                act.activation(rwork[:, 8 * i:8 * i + 8], rwork[:, 8 * i:8 * i + 8], ACT.Exp,
                               accum_out=rwork[:, 32 + i:33 + i]).then_inc(S("r_exp"), 1)
                act.wait_ge(S("r_e"), i + 1)
                act.activation(rwork[:, 40 + i:41 + i], rwork[:, 40 + i:41 + i], ACT.Exp).then_inc(S("r_exp2"), 1)
            if stop <= 1:
                return
            def split_half(m, h, i, turn):
                k = 2 * m + h
                act.wait_ge(m_arr[k], 16 * i + 16 * turn if i is not None else 16 * turn)
                act.activation(m_whi[:, k, :], m_raw[:, k, :], ACT.Copy).then_inc(m_hi[m], 1)

            def rows_hi():
                act.activation(m_xh[:, :, :], XTb[:, 0:DC * BLK].rearrange("p (a b) -> p a b", a=DC),
                               ACT.Copy).then_inc(m_xhi, 1)

            def act_hi():
                act.activation(m_ah[:, :, :], ATb[:, 0:4 * BLK].rearrange("p (a b) -> p a b", a=4),
                               ACT.Copy).then_inc(m_ahi, 1)

            def y_out():
                act.activation(y_b[:, 0:512], Y0b[0:BLK, :], ACT.Copy)
                act.activation(y_b[:, 512:1024], Y1b[0:BLK, :], ACT.Copy).then_inc(m_y, 1)

            act.sem_inc(m_y, 1)
            for m in (0, 1):
                for h in range(2):
                    split_half(m, h, None, 1)
            act.wait_ge(m_ready, 1)
            count = act.value_load(blk[0:1, NX:NX + 1], min_val=NE - 2, max_val=NBLK - 2)
            act.wait_ge(m_filled["xT"], 1)
            rows_hi()
            act.wait_ge(m_filled["h1"], 1)
            act.activation(silu_b, H1b[0:BLK, :], ACT.Silu).then_inc(m_silu, 1)
            act.wait_ge(m_filled["xT"], 2)
            rows_hi()
            for h in range(2):
                split_half(0, h, None, 2)

            def act_block(i, last):
                act.wait_ge(m_filled["h3"], i + 1)
                for h in range(2):
                    split_half(1, h, i, 2)
                act.wait_ge(m_filled["aT"], i + 1)
                act_hi()
                act.wait_ge(m_filled["h1"], i + 2)
                act.wait_ge(m_act, i + 1)
                act.activation(silu_b, H1b[0:BLK, :], ACT.Silu).then_inc(m_silu, 1)
                for h in range(2):
                    split_half(2, h, i, 1)
                if not last:
                    act.wait_ge(m_filled["xT"], i + 3)
                    rows_hi()
                    for h in range(2):
                        split_half(0, h, i, 3)
                act.wait_ge(m_filled["y"], i + 1)
                act.wait_ge(m_scatter, 16 * i + 16)
                y_out()

            with act.Fori(0, count) as i:
                act_block(i, False)
            act_block(count, True)
            act.wait_ge(m_filled["aT"], count + 2)
            act_hi()
            for h in range(2):
                split_half(2, h, count, 2)
            act.wait_ge(m_filled["y"], count + 2)
            act.wait_ge(m_scatter, 16 * count + 32)
            y_out()
            if stop <= 2:
                return
            act.wait_ge(m_done, 1)
            hi_at.limit = len(order)
            row(side[:, 0:1024], "final_norm", D, S("w_fin"))
            act.dma_start(scratch[:, 0:2048], a["decays"]).then_inc(S("w_dec"), 16)
            act.wait_ge(S("pos2free"), 1)
            row(scratch[:, 3584:4096].bitcast(I32), "positions_2", T, S("w_pos2"))
            hi_until(act, n_first + 1)
            act_sumsq(act, chain, "n3", lambda i: x[:, i, :], NT, arena[:, 8192:8192 + D], ssq,
                      lambda i: act.wait_ge(S("x2pre"), i + 1))
            act_sqrt(act, "n3", rstd, NT)
            act_sumsq(act, chain, "n4", lambda i: x[:, i, :], NT, arena[:, 8192:8192 + D], ssq2,
                      lambda i: act.wait_ge(S("x2"), i + 1))
            act_sqrt(act, "n4", rstd2, NT)
            act_split_jobs(act, "hT3", hTh, lambda c: PRM("pre_mix", c))
            act_second(act, chain, row)

        @block.tensor
        def _(pe):
            pe.wait_ge(s_const, 64)
            pe.wait_ge(S("xn1"), NT)
            pe_to_feature(pe, J["hT1"], lambda i, c: xn(i)[:, P * c:P * (c + 1)])
            read(pe, J["hT1"])
            pe.wait_ge(S("wf_lo"), 1)
            job = J["zT"][0]
            for c in range(DC):
                mm = three(pe, banks[job.bank][0:H1, :], (wf_h[:, c, :], wf_l[:, c, :]), (hT[0](c), hT[1](c)),
                           c == 0, c == DC - 1)
            fill(mm, job)
            pe_feature(pe, "qs", hT)
            read(pe, J["zT"])
            job = J["flog"][0]
            claim(pe, job)
            for i in range(NT):
                mm = pe.transpose(banks[job.bank][:, H1 * i:H1 * (i + 1)], zT[:, P * i:P * (i + 1)], ident[0:H1, 0:H1])
            fill(mm, job)
            pe_feature(pe, "ks", hT)
            pe_feature(pe, "qf", hT)
            read(pe, J["qs"] + J["ks"])
            for c, job in enumerate(J["qs_rot"]):
                claim(pe, job)
                fill(pe.matmul(banks[job.bank][:, :], C("rot_swa"), qsT[:, c, :], start=True, stop=True), job)
            for c, job in enumerate(J["ks_rot"]):
                claim(pe, job)
                fill(pe.matmul(banks[job.bank][:, :], C("rot_swa"), ksT[:, c, :], start=True, stop=True), job)
            pe_feature(pe, "kf", hT)
            pe.wait_ge(S("logf"), 1)
            job = J["cT"][0]
            claim(pe, job)
            for i in range(NT):
                mm = pe.matmul(banks[job.bank][0:H1, P * i:T], logf[:, i, :], C("upto")[:, 0:T - P * i],
                               start=(i == 0), stop=(i == NT - 1))
            fill(mm, job)
            u = units_of["vs"][0]
            loaded(pe, u)
            wh, wl = parts(u)
            for i, job in enumerate(J["vs"]):
                claim(pe, job)
                t = slice(P * i, P * (i + 1))
                for c in range(DC):
                    mm = three(pe, banks[job.bank][:, 0:P], (hTh[:, c, t], hTl[:, c, t]), (wh[:, c, :], wl[:, c, :]),
                               c == 0, c == DC - 1)
                fill(mm, job)
            pe_token(pe, "vf", hT)
            read(pe, J["cT"] + J["qf"] + J["kf"] + J["vf"])

            def decay(t):
                if t % NT == 0:
                    h = t // NT
                    job = J["decay"][h]
                    claim(pe, job)
                    fill(pe.matmul(banks[job.bank][:, :], ident[0:H1, h:h + 1].broadcast_to([H1, P]), cT, start=True,
                                   stop=True), job)

            pe_attention(pe, FOX, decay)

            def heads_to_feature(name, A, o):
                read(pe, A.jv)
                pe_to_feature(pe, J[name], lambda i, c: o[:, i, P * c:P * (c + 1)])

            read(pe, J["qs_rot"] + J["ks_rot"] + J["vs"])
            pe_attention(pe, SWA)
            heads_to_feature("swa_oT", SWA, o_swa)
            heads_to_feature("fox_oT", FOX, o_fox)
            pe_feature(pe, "gf", hT)
            pe_feature(pe, "gs", hT)
            read(pe, J["fox_oT"] + J["swa_oT"])
            pe_feature(pe, "pf", ofT)
            pe_feature(pe, "ps", osT)
            pe.wait_ge(S("merged_lo"), DC)
            for n in range(2):
                pe_token(pe, f"out{n}", hT)
            pe.wait_ge(S("h2"), NT)
            pe_to_feature(pe, J["hT2"], lambda i, c: h2[:, i, P * c:P * (c + 1)])
            read(pe, J["hT2"])
            pe.wait_ge(S("w_r"), 96)
            for i, job in enumerate(J["router"]):
                claim(pe, job)
                for c in range(DC):
                    mm = pe.matmul(banks[job.bank][:, 0:NR], h2T[:, c, P * i:P * (i + 1)], w_r[:, c, :],
                                   start=(c == 0), stop=(c == DC - 1))
                fill(mm, job)
            for i, job in enumerate(J["rank"]):
                claim(pe, job)
                pe.wait_ge(S("r_both"), i + 1)
                for j in range(i):
                    pe.matmul(banks[job.bank][:, 0:NE], C("ones"), both[:, j, :], start=(j == 0), stop=False)
                fill(pe.matmul(banks[job.bank][:, 0:NE], C("before"), both[:, i, :], start=(i == 0), stop=True), job)
            job = J["count"][0]
            claim(pe, job)
            for j in range(NT):
                mm = pe.matmul(banks[job.bank][0:NE, 0:1], both[:, j, :], C("ones")[:, 0:1], start=(j == 0),
                               stop=(j == NT - 1))
            fill(mm, job)
            job = J["starts"][0]
            claim(pe, job)
            pe.wait_ge(S("r_over"), 1)
            over = rwork[0:NE, 257:258]
            pe.matmul(banks[job.bank][0:NE, 0:1], C("before")[0:NE, 0:NE], over, start=True, stop=True)
            fill(pe.matmul(banks[job.bank][0:NE, 1:2], C("ones")[0:NE, 0:NE], over, start=True, stop=True), job)
            job = J["further"][0]
            claim(pe, job)
            pe.wait_ge(S("r_further"), 1)
            fill(pe.matmul(banks[job.bank][0:1, 0:SPILL], C("ones")[0:NE, 0:1],
                           rwork[0:NE, 320 + 2 * SPILL:320 + 3 * SPILL], start=True, stop=True), job)
            pe.wait_ge(S("ids_f"), 1)
            for k, job in enumerate(J["ids"]):
                claim(pe, job)
                for j in range(4):
                    mm = pe.transpose(banks[job.bank][0:BLK, P * j:P * (j + 1)], ids_f[:, 4 * k + j, :], ident)
                fill(mm, job)
            if stop <= 1:
                return
            for job in J["before_moe"]:
                claim(pe, job)
            pe.wait_ge(m_ready, 1)
            count = pe.value_load(blk[0:1, NX:NX + 1], min_val=NE - 2, max_val=NBLK - 2)

            def rows_to_columns():
                pe.sem_inc(m_pe_go, 1)
                for c in range(DC):
                    mm = pe.transpose(XTb[:, BLK * c:BLK * (c + 1)], Xe[:, c:D:DC], ident[0:BLK, 0:BLK])
                mm.then_inc(m_filled["xT"], 1)

            def acts_to_columns():
                pe.sem_inc(m_pe_go, 1)
                for c in range(4):
                    mm = pe.transpose(ATb[:, BLK * c:BLK * (c + 1)], act_b[:, c:DE:4], ident[0:BLK, 0:BLK])
                mm.then_inc(m_filled["aT"], 1)

            def times(m, bank, i, turn, name):
                for h in range(2):
                    pe.wait_ge(m_lo[m], 2 * i + 2 * turn + h + 1 if i is not None else h + 1)
                    wh = m_whi[:, 2 * m + h, :].rearrange("p (c n) -> p c n", c=4)
                    wl = m_wlo[:, 2 * m + h, :].rearrange("p (c n) -> p c n", c=4)
                    for c in range(4):
                        k = 4 * h + c
                        for j, (xa, w) in enumerate(((m_xh, wh), (m_xl, wh), (m_xh, wl))):
                            mm = pe.matmul(bank[0:BLK, :], xa[:, k, :], w[:, c, :], start=(k == 0 and j == 0),
                                           stop=(k == DC - 1 and j == 2))
                mm.then_inc(m_filled[name], 1)

            def times_w2(i, turn):
                for h in range(2):
                    pe.wait_ge(m_lo[2], 2 * i + 2 * turn + h + 3)
                    wh = m_whi[:, 4 + h, :].rearrange("p (c n) -> p c n", c=2)
                    wl = m_wlo[:, 4 + h, :].rearrange("p (c n) -> p c n", c=2)
                    for c in range(2):
                        k = 2 * h + c
                        for n, bank in enumerate((Y0b, Y1b)):
                            for j, (xa, w) in enumerate(((m_ah, wh), (m_al, wh), (m_ah, wl))):
                                mm = pe.matmul(bank[0:BLK, :], xa[:, k, :], w[:, c, 512 * n:512 * (n + 1)],
                                               start=(k == 0 and j == 0), stop=(k == 3 and j == 2))
                mm.then_inc(m_filled["y"], 1)

            pe.wait_ge(m_gather, 16)
            rows_to_columns()
            pe.wait_ge(m_x, 1)
            times(0, H1b, None, 0, "h1")
            times(1, H3b, None, 0, "h3")
            pe.wait_ge(m_gather, 32)
            rows_to_columns()

            def pe_block(i, last):
                pe.wait_ge(m_x, i + 2)
                pe.wait_ge(m_silu, i + 1)
                times(0, H1b, i, 1, "h1")
                pe.wait_ge(m_act, i + 1)
                acts_to_columns()
                times(1, H3b, i, 1, "h3")
                if not last:
                    pe.wait_ge(m_gather, 16 * i + 48)
                    rows_to_columns()
                pe.wait_ge(m_a, i + 1)
                pe.wait_ge(m_y, i + 1)
                times_w2(i, 0)

            with pe.Fori(0, count) as i:
                pe_block(i, False)
            pe_block(count, True)
            pe.wait_ge(m_act, count + 2)
            acts_to_columns()
            pe.wait_ge(m_a, count + 2)
            pe.wait_ge(m_y, count + 2)
            times_w2(count, 1)
            pe.wait_ge(m_y, count + 3)
            pe.wait_ge(m_x, count + 2)
            for job in J["before_moe"]:
                pe.sem_inc(filled[job.bank], 1)
                pe.sem_inc(freed[job.bank], 1)
            if stop <= 2:
                return
            pe_second(pe, heads_to_feature)

        @block.vector
        def _(v):
            chain = Chain(v, dve_own)
            v.wait_ge(s_const, 64)
            chain(v.tensor_scalar(nsink, sink_row, -1.0, None, ALU.mult))
            dve_rstd(v, chain, "n1", ssq, rstd, NT, D)
            for i in range(NT):
                v.wait_ge(s_x[i], 16)
                v.tensor_scalar(xn(i), x[:, i, :], rstd[:, i:i + 1], None, ALU.mult).then_inc(S("xn1"), 1)

            def evac(name, dst, parity=None, scale=None):
                for c, job in enumerate(J[name]):
                    if parity is None or c % 2 == parity:
                        full(v, job)
                        if scale is None:
                            free(v.tensor_copy(dst[:, c, :], banks[job.bank][:, :]), job)
                        else:
                            free(v.tensor_scalar(dst[:, c, :], banks[job.bank][:, :], scale(c), None, ALU.mult), job)

            lo_until(v, 0)
            dve_split_jobs(v, "hT1", hTh, hTl, lambda c: PRM("attn_norm", c))
            dve_split(v, "w_f", wf_l[:, :, :], w_f, wf_h[:, :, :]).then_inc(S("wf_lo"), 1)
            lo_until(v, 1)
            v.wait_ge(s_pos, 16)
            chain(v.tensor_copy(posf, pos_i))
            dve_angles(v, chain, "rope1", C("inv_swa"), cos1, sin1, posf, ang, red)
            v.sem_inc(S("posdone"), 1)
            ahead(lo_until, v, "qs", W1C - 1)
            job = J["flog"][0]
            full(v, job)
            pv = banks[job.bank][:, 0:H1 * NT].rearrange("p (i h) -> p i h", h=H1)
            for i in range(NT):
                ins = v.tensor_tensor(logf_z[:, i, :], pv[:, i, :], bf_row, ALU.add)
                if i == NT - 1:
                    free(ins, job)
            read(v, [job])
            chain(v.scalar_tensor_tensor(logf_t, logf_z, -1.0, logf_z, ALU.mult, ALU.max))
            v.sem_inc(S("f_abs"), 1)
            v.wait_ge(S("f_exp"), 1)
            chain(v.tensor_scalar(logf_t, logf_t, 1.0, None, ALU.add))
            v.sem_inc(S("f_one"), 1)
            v.wait_ge(S("f_ln"), 1)
            chain(v.tensor_scalar(logf_z, logf_z, 0.0, None, ALU.min))
            v.tensor_tensor(logf, logf_z, logf_t, ALU.subtract).then_inc(S("logf"), 1)
            for g, job in enumerate(J["ks"]):
                ahead(lo_until, v, "ks", g)
                full(v, job)
                free(v.tensor_copy(ksT[:, g, :], banks[job.bank][:, :]), job)
            lo_until(v, units_of["kf"][0].n)
            v.wait_ge(S("sines"), 2)
            read(v, J["qs"] + J["ks"])
            for c, job in enumerate(J["qs_rot"]):
                dve_rope(v, chain, job, qsT[:, c, :], cos1, sin1, tmp[c % 2])
            for c, job in enumerate(J["ks_rot"]):
                dve_rope(v, chain, job, ksT[:, c, :], cos1, sin1, tmp[c % 2])
            for c, job in enumerate(J["kf"]):
                ahead(lo_until, v, "kf", c)
                full(v, job)
                free(v.tensor_copy(kfT[:, c, :], banks[job.bank][:, :]), job)
            ahead(lo_until, v, "vf")
            lo_until(v, units_of["gf"][0].n)

            def decay(t):
                if t % NT == 0:
                    read(v, [J["decay"][t // NT]])

            lo_until(v, units_of["gf"][1].n)
            dve_attention(v, FOX, chain, decay)
            read(v, FOX.jv)
            dve_attention(v, SWA, chain)
            dve_split_jobs(v, "swa_oT", osTh, osTl)
            dve_split_jobs(v, "fox_oT", ofTh, ofTl)
            for name in ("gf", "gs"):
                ahead(lo_until, v, name, DC - 1)
            read(v, J["gf"] + J["gs"])
            for c, job in enumerate(J["pf"]):
                ahead(lo_until, v, "pf", c)
                full(v, job)
                free(v.tensor_tensor(gfT[:, c, :], gfT[:, c, :], banks[job.bank][:, :], ALU.mult), job)
            for c, job in enumerate(J["ps"]):
                ahead(lo_until, v, "ps", c)
                full(v, job)
                free(v.tensor_tensor(gsT[:, c, :], gsT[:, c, :], banks[job.bank][:, :], ALU.mult), job)
                read(v, [J["pf"][c], job])
                v.tensor_tensor(gfT[:, c, :], gfT[:, c, :], gsT[:, c, :], ALU.add).then_inc(S("merged"), 1)
            for c in range(DC):
                dve_split(v, ("merged", c), hTl[:, c, :], gfT[:, c, :], hTh[:, c, :]).then_inc(S("merged_lo"), 1)
            for n in range(2):
                ahead(lo_until, v, f"out{n}")
                for i, job in enumerate(J[f"out{n}"]):
                    full(v, job)
                    xs = x[:, i, 512 * n:512 * (n + 1)]
                    ins = v.tensor_tensor(xs, xs, banks[job.bank][:, :], ALU.add)
                    free(ins, job)
            read(v, J["out0"] + J["out1"])
            v.sem_inc(S("x1"), 2 * NT)
            dve_rstd(v, chain, "n2", ssq, rstd, NT, D)
            v.wait_ge(S("w_r"), 96)
            for i in range(NT):
                v.scalar_tensor_tensor(h2[:, i, :], x[:, i, :], rstd[:, i:i + 1], row_gain, ALU.mult,
                                       ALU.mult).then_inc(S("h2"), 1)
            evac("hT2", h2T, 1)
            def split_half(m, h, value):
                k = 2 * m + h
                v.wait_ge(m_hi[m], value)
                v.tensor_tensor(m_wlo[:, k, :], m_raw[:, k, :], m_whi[:, k, :].bitcast(F32),
                                ALU.subtract).then_inc(m_lo[m], 1)

            def first_expert():
                v.sem_inc(m_lo[2], 2)
                v.wait_ge(S("hrows"), 16)
                for m in (0, 1):
                    for h in range(2):
                        split_half(m, h, h + 1)

            dve_route(v, chain, first_expert)
            if stop <= 1:
                return
            def rows_lo():
                v.tensor_tensor(m_xl[:, :, :], XTb[:, 0:DC * BLK].rearrange("p (a b) -> p a b", a=DC),
                                m_xh[:, :, :].bitcast(F32), ALU.subtract).then_inc(m_x, 1)

            def act_lo():
                v.tensor_tensor(m_al[:, :, :], ATb[:, 0:4 * BLK].rearrange("p (a b) -> p a b", a=4),
                                m_ah[:, :, :].bitcast(F32), ALU.subtract).then_inc(m_a, 1)

            def activate():
                v.tensor_tensor(act_b, silu_b, H3b[0:BLK, :], ALU.mult).then_inc(m_act, 1)

            count = v.value_load(blk[0:1, NX:NX + 1], min_val=NE - 2, max_val=NBLK - 2)
            v.wait_ge(m_xhi, 1)
            rows_lo()
            v.wait_ge(m_silu, 1)
            v.wait_ge(m_filled["h3"], 1)
            activate()
            v.wait_ge(m_xhi, 2)
            rows_lo()
            for h in range(2):
                split_half(0, h, h + 3)

            def dve_block(i, last):
                for h in range(2):
                    split_half(1, h, 2 * i + (h + 3))
                v.wait_ge(m_ahi, i + 1)
                act_lo()
                for h in range(2):
                    split_half(2, h, 2 * i + (h + 1))
                if not last:
                    v.wait_ge(m_xhi, i + 3)
                    rows_lo()
                v.wait_ge(m_silu, i + 2)
                v.wait_ge(m_filled["h3"], i + 2)
                activate()
                if not last:
                    for h in range(2):
                        split_half(0, h, 2 * i + (h + 5))

            with v.Fori(0, count) as i:
                dve_block(i, False)
            dve_block(count, True)
            v.wait_ge(m_ahi, count + 2)
            act_lo()
            for h in range(2):
                split_half(2, h, 2 * count + (h + 3))
            if stop <= 2:
                return
            v.wait_ge(m_done, 1)
            lo_at.limit = len(order)
            for i in range(NT):
                v.wait_ge(S(f"y_back{i}"), 16)
                y = ring_y(i)
                for k in range(2):
                    ins = v.scalar_tensor_tensor(x[:, i, :], y[:, k, :], gates[:, i, k:k + 1], x[:, i, :], ALU.mult, ALU.add)
                    if k == 0:
                        chain(ins)
                    else:
                        ins.then_inc(S("x2pre"), 1)
            dve_rstd(v, chain, "n3", ssq, rstd, NT, D)
            v.wait_ge(S("w_fin"), 16)
            for i in range(NT):
                v.scalar_tensor_tensor(x[:, i, :], x[:, i, :], rstd[:, i:i + 1], side[:, 0:1024], ALU.mult,
                                       ALU.mult).then_inc(S("x2"), 1)
            v.sem_inc(S("n3x"), NT)
            lo_until(v, n_first + 1)
            dve_rstd(v, chain, "n4", ssq2, rstd2, NT, D)
            v.wait_ge(S("x2"), NT)
            for i in range(NT):
                v.tensor_scalar(xn(i), x[:, i, :], rstd2[:, i:i + 1], None, ALU.mult).then_inc(S("xn4"), 1)
            dve_split_jobs(v, "hT3", hTh, hTl, lambda c: PRM("pre_mix", c))
            dve_second(v, chain, evac)

        @block.gpsimd
        def _(pool):
            chain = Chain(pool, pool_own)
            pool.wait_ge(S("x1"), 2 * NT)
            chain(pool.memset(sentinel, NOTHING))
            chain(pool.memset(Xe, 0.0))
            pool.dma_start(slot_ids.rearrange("(p n) o -> p (n o)", p=P), sentinel).then_inc(m_scatter, 16)
            pool.wait_ge(S("h2"), NT)
            pool.dma_start(h_rows.rearrange("(i p) n -> p i n", p=P), h2).then_inc(S("hrows"), 16)
            pool.wait_ge(m_scatter, 16)
            pool.wait_ge(S("r_pos"), 2 * NT)
            pool.wait_ge(S("r_id"), 1)
            for n in range(2 * NT):
                pool.indirect_dma_start(slot_ids, bass.IndirectOffsetOnAxis(ap=pos_t[:, n:n + 1].bitcast(U32), axis=0),
                                        id_t[:, n:n + 1], None, bounds_check=NE * T - 1,
                                        oob_is_err=False).then_inc(S("ids_out"), 16)
            pool.wait_ge(S("ids_out"), 32 * NT)
            pool.dma_start(ids_raw, slot_ids.rearrange("(k p n) o -> p k (n o)", k=8, p=P)).then_inc(S("ids_in"), 16)
            if stop <= 1:
                return
            pool.wait_ge(S("hrows"), 16)
            pool.wait_ge(m_ready, 1)
            count = pool.value_load(blk[0:1, NX:NX + 1], min_val=NE - 2, max_val=NBLK - 2)
            last_token, last_row = pool.to_reg(T - 1), pool.to_reg(2 * T - 1)

            def gather():
                pool.indirect_dma_start(Xe, None, h_rows, bass.IndirectOffsetOnAxis(ap=idx_t.bitcast(U32), axis=0),
                                        bounds_check=last_token, oob_is_err=False).then_inc(m_gather, 16)

            def scatter():
                pool.indirect_dma_start(y_rows, bass.IndirectOffsetOnAxis(ap=idx_a.bitcast(U32), axis=0), y_b, None,
                                        bounds_check=last_row, oob_is_err=False).then_inc(m_scatter, 16)

            for b in range(2):
                if b:
                    pool.wait_ge(m_gather, 16)
                pool.tensor_copy(idx_t, tok_tab[:, EB * b:EB * b + 1]).then_inc(m_idx, 1)
                if b:
                    pool.wait_ge(m_filled["xT"], 1)
                pool.wait_ge(m_idx, b + 1)
                gather()

            def pool_block(i, last):
                col0 = pool.value_load(blk[0:1, bass.ds(i, 1)], min_val=0, max_val=NE * EB - 1)
                if not last:
                    col = pool.value_load(blk[0:1, bass.ds(i + 2, 1)], min_val=0, max_val=NE * EB - 1)
                    pool.wait_ge(m_gather, 16 * i + 32)
                    pool.tensor_copy(idx_t, tok_tab[:, bass.ds(col, 1)]).then_inc(m_idx, 1)
                    pool.wait_ge(m_filled["xT"], i + 2)
                    pool.wait_ge(m_idx, 2 * i + 3)
                    pool.sem_inc(m_go, 1)
                    gather()
                pool.wait_ge(m_scatter, 16 * i + 16)
                pool.tensor_copy(idx_a, asg_tab[:, bass.ds(col0, 1)]).then_inc(m_idx, 1)
                pool.wait_ge(m_idx, 2 * i + (3 if last else 4))
                pool.wait_ge(m_y, i + 2)
                pool.sem_inc(m_go, 1)
                scatter()

            with pool.Fori(0, count) as i:
                pool_block(i, False)
            pool_block(count, True)
            col0 = pool.value_load(blk[0:1, bass.ds(count + 1, 1)], min_val=0, max_val=NE * EB - 1)
            pool.wait_ge(m_scatter, 16 * count + 32)
            pool.tensor_copy(idx_a, asg_tab[:, bass.ds(col0, 1)]).then_inc(m_idx, 1)
            pool.wait_ge(m_idx, 2 * count + 4)
            pool.wait_ge(m_y, count + 3)
            pool.sem_inc(m_go, 1)
            scatter()
            pool.wait_ge(m_gather, 16 * count + 32)
            pool.wait_ge(m_scatter, 16 * count + 48)
            pool.sem_inc(m_done, 1)
            if stop <= 2:
                return
            pool.sem_inc(S("pos2free"), 1)
            for i in range(NT):
                pool.dma_start(ring_y(i), y_rows[2 * P * i:2 * P * (i + 1), :].rearrange("(p k) n -> p k n", k=2))\
                    .then_inc(S(f"y_back{i}"), 16)

    return nc


INPUTS = ["x", "positions", "w_in", "b_forget", "attn_sinks", "w_proj_fox", "w_proj_swa", "w_out", "ffn_norm",
          "w_group", "b_group", "w_expert", "b_expert", "w1", "w3", "w2", "final_norm", "p_2", "positions_2", "w_in_2",
          "w_uq_2", "w_ukv_2", "w_o_2", "post_mix_norm_2", "w_gate_2", "w_up_2", "w_down_2", "post_ffn_norm_2",
          "w_ple_proj_2", "ple_norm_2", "w_ple_gate_2", "b_ple_gate_2"]


def arrays_of(inputs):
    arrays = {n: np.ascontiguousarray(inputs[n]) for n in INPUTS}
    arrays["consts"] = constants()
    arrays["decays"] = late_constants()
    arrays["route_consts"] = route_constants()
    arrays["params"] = params(inputs)
    return arrays


def kernel(**inputs):
    import concourse.bacc as bacc
    from concourse.bass_utils import run_bass_kernel_spmd

    arrays = arrays_of(inputs)
    nc = bacc.Bacc("TRN2", target_bir_lowering=False, num_devices=1)
    aps = {n: nc.dram_tensor("in_" + n, v.shape, mybir.dt.from_np(v.dtype), kind="ExternalInput").ap()
           for n, v in arrays.items()}
    out = nc.dram_tensor("out_0", (1, T, D), F32, kind="ExternalOutput").ap()
    build(nc, aps, out)
    r = run_bass_kernel_spmd(nc, [{"in_" + n: v for n, v in arrays.items()}], core_ids=[0])
    return r.results[0]["out_0"]
```
